# Optimizing a Trainium2 kernel written in Bass

```python
import math, functools
import jax, jax.numpy as jnp
from jax import lax
import numpy as np

D_MODEL = 1024
BATCH = 1
SEQ = 1024
DEPTH = 1
DEC_BATCH = 8
DEC_SEQ = 1
PAST_LEN = 8192
PAGE_SIZE = 128

N_META = 16
MIX_WIDTH = D_MODEL
CONV_CH = MIX_WIDTH // 2
CONV_WIDTH = 3
RET_HEADS = 4
QK_DIM = (MIX_WIDTH // 2) // RET_HEADS
V_DIM = (MIX_WIDTH // 2) // RET_HEADS
RET_WIDTH = RET_HEADS * V_DIM
CHUNK = 128
D_FF = 4 * D_MODEL
ROPE_BASE = 10000.0
EPS = 1e-6
IN_WIDTHS = (CONV_CH, CONV_CH, CONV_CH, RET_HEADS * QK_DIM, RET_HEADS * QK_DIM, RET_WIDTH, RET_WIDTH)
IN_TOTAL = sum(IN_WIDTHS)
SPLITS = tuple(int(s) for s in np.cumsum(IN_WIDTHS)[:-1])

kernel_name = "hymba_conv_retention_decode_step"

def rmsnorm(x, g):
    xf = x.astype(jnp.float32)
    y = xf * lax.rsqrt(jnp.mean(xf * xf, axis=-1, keepdims=True) + EPS)
    return (y * g.astype(jnp.float32)).astype(x.dtype)

def head_rmsnorm(o):
    of = o.astype(jnp.float32)
    y = of * lax.rsqrt(jnp.mean(of * of, axis=-1, keepdims=True) + EPS)
    return y.astype(o.dtype)

def rotary(x, pos):
    dh = x.shape[-1]
    inv_freq = 1.0 / (ROPE_BASE ** (jnp.arange(0, dh, 2, dtype=jnp.float32) / dh))
    ang = pos[:, None] * inv_freq[None, :]
    cos = jnp.cos(ang)[None, :, None, :].astype(x.dtype)
    sin = jnp.sin(ang)[None, :, None, :].astype(x.dtype)
    x1, x2 = jnp.split(x, 2, axis=-1)
    return jnp.concatenate([x1 * cos - x2 * sin, x1 * sin + x2 * cos], axis=-1)

def causal_conv3(u_prev, u, w):
    full = jnp.concatenate([u_prev.astype(u.dtype), u], axis=1)
    y = w[0] * full[:, :-2] + w[1] * full[:, 1:-1] + w[2] * full[:, 2:]
    return y, full[:, -(CONV_WIDTH - 1):]

def retention_block(q, k, v, s_prev, log_gamma):
    L = q.shape[1]
    idx = jnp.arange(L, dtype=jnp.float32)
    diff = idx[:, None] - idx[None, :]
    decay = jnp.where(diff >= 0,
                      jnp.exp(log_gamma[:, None, None] * jnp.maximum(diff, 0.0)),
                      0.0).astype(q.dtype)
    scores = jnp.einsum('bihd,bjhd->bhij', q, k) * decay
    inner = jnp.einsum('bhij,bjhe->bihe', scores, v)
    q_decay = jnp.exp((idx[:, None] + 1.0) * log_gamma[None, :]).astype(q.dtype)
    cross = jnp.einsum('bihd,bhde->bihe', q, s_prev) * q_decay[None, :, :, None]
    k_decay = jnp.exp((L - 1.0 - idx)[:, None] * log_gamma[None, :]).astype(q.dtype)
    s_new = (s_prev * jnp.exp(L * log_gamma).astype(q.dtype)[None, :, None, None]
             + jnp.einsum('bjhd,bjhe->bhde', k * k_decay[None, :, :, None], v))
    return inner + cross, s_new

def retention_prompt(q, k, v, s_prev, log_gamma):
    o_meta, s = retention_block(q[:, :N_META], k[:, :N_META], v[:, :N_META], s_prev, log_gamma)
    Bsz, T, H, dk = q.shape
    n_chunks = (T - N_META) // CHUNK

    def to_chunks(a):
        a = a[:, N_META:].reshape(Bsz, n_chunks, CHUNK, H, a.shape[-1])
        return jnp.moveaxis(a, 1, 0)

    def step(s_c, blk):
        qc, kc, vc = blk
        o_c, s_n = retention_block(qc, kc, vc, s_c, log_gamma)
        return s_n, o_c

    s_final, o_chunks = lax.scan(step, s, (to_chunks(q), to_chunks(k), to_chunks(v)))
    o_real = jnp.moveaxis(o_chunks, 0, 1).reshape(Bsz, n_chunks * CHUNK, H, v.shape[-1])
    return jnp.concatenate([o_meta, o_real], axis=1), s_final

def layer(h, pos, conv_prev, ret_prev, norm_mix, w_in, conv_w, w_out,
          norm_mlp, w_up, w_down, ret_fn):
    Bsz, T, _ = h.shape
    hn = rmsnorm(h, norm_mix)
    z = hn @ w_in
    u_in, c_gate, b_gate, q, k, v, g = jnp.split(z, SPLITS, axis=-1)
    conv_y, conv_state = causal_conv3(conv_prev, c_gate * u_in, conv_w)
    y_conv = b_gate * conv_y
    q = rotary(q.reshape(Bsz, T, RET_HEADS, QK_DIM), pos)
    k = rotary(k.reshape(Bsz, T, RET_HEADS, QK_DIM), pos) * (QK_DIM ** -0.5)
    v = v.reshape(Bsz, T, RET_HEADS, V_DIM)
    o, ret_state = ret_fn(q, k, v, ret_prev.astype(q.dtype))
    y_ret = head_rmsnorm(o).reshape(Bsz, T, RET_WIDTH) * jax.nn.silu(g)
    h = h + jnp.concatenate([y_conv, y_ret], axis=-1) @ w_out
    hn2 = rmsnorm(h, norm_mlp)
    h = h + jnp.square(jax.nn.relu(hn2 @ w_up)) @ w_down
    return h, conv_state, ret_state

def setup_inputs(seed: int = 0) -> dict:
    key = jax.random.key(seed)
    ks = jax.random.split(key, 16)
    f32 = jnp.float32
    return {
        "x_prompt": jax.random.normal(ks[0], (BATCH, SEQ, D_MODEL), f32),
        "x_sample": jax.random.normal(ks[1], (DEC_BATCH, DEC_SEQ, D_MODEL), f32),
        "cache_conv": jax.random.normal(ks[2], (DEPTH, DEC_BATCH, CONV_WIDTH - 1, CONV_CH), f32),
        "state_ret": 0.5 * jax.random.normal(ks[3], (DEPTH, DEC_BATCH, RET_HEADS, QK_DIM, V_DIM), f32),
        "meta_tokens": jax.random.normal(ks[4], (N_META, D_MODEL), f32),
        "norm_mix": 1.0 + 0.02 * jax.random.normal(ks[5], (DEPTH, D_MODEL), f32),
        "w_in": jax.random.normal(ks[6], (DEPTH, D_MODEL, IN_TOTAL), f32) * D_MODEL ** -0.5,
        "conv_w": jax.random.normal(ks[7], (DEPTH, CONV_WIDTH, CONV_CH), f32) * CONV_WIDTH ** -0.5,
        "w_out": jax.random.normal(ks[8], (DEPTH, MIX_WIDTH, D_MODEL), f32) * MIX_WIDTH ** -0.5,
        "norm_mlp": 1.0 + 0.02 * jax.random.normal(ks[9], (DEPTH, D_MODEL), f32),
        "w_up": jax.random.normal(ks[10], (DEPTH, D_MODEL, D_FF), f32) * D_MODEL ** -0.5,
        "w_down": jax.random.normal(ks[11], (DEPTH, D_FF, D_MODEL), f32) * D_FF ** -0.5,
        "norm_final": 1.0 + 0.02 * jax.random.normal(ks[12], (D_MODEL,), f32),
    }

def reference(x_prompt, x_sample, cache_conv, state_ret, meta_tokens, norm_mix, w_in,
              conv_w, w_out, norm_mlp, w_up, w_down, norm_final):
    log_gamma = jnp.log(1.0 - 2.0 ** (-5.0 - jnp.arange(RET_HEADS, dtype=jnp.float32)))
    ret_prompt_fn = functools.partial(retention_prompt, log_gamma=log_gamma)
    ret_sample_fn = functools.partial(retention_block, log_gamma=log_gamma)

    meta = jnp.broadcast_to(meta_tokens.astype(x_prompt.dtype)[None], (BATCH, N_META, D_MODEL))
    hp = jnp.concatenate([meta, x_prompt], axis=1)
    pos_p = jnp.arange(SEQ + N_META, dtype=jnp.float32)
    hs = x_sample
    pos_s = PAST_LEN + jnp.arange(DEC_SEQ, dtype=jnp.float32)

    conv_zero = jnp.zeros((BATCH, CONV_WIDTH - 1, CONV_CH), x_prompt.dtype)
    ret_zero = jnp.zeros((BATCH, RET_HEADS, QK_DIM, V_DIM), x_prompt.dtype)
    conv_p_list, ret_p_list, conv_s_list, ret_s_list = [], [], [], []
    for l in range(DEPTH):
        hp, cp, rp = layer(hp, pos_p, conv_zero, ret_zero, norm_mix[l], w_in[l], conv_w[l],
                           w_out[l], norm_mlp[l], w_up[l], w_down[l], ret_prompt_fn)
        hs, cs, rs = layer(hs, pos_s, cache_conv[l], state_ret[l], norm_mix[l], w_in[l], conv_w[l],
                           w_out[l], norm_mlp[l], w_up[l], w_down[l], ret_sample_fn)
        conv_p_list.append(cp); ret_p_list.append(rp)
        conv_s_list.append(cs); ret_s_list.append(rs)

    y_prompt = rmsnorm(hp, norm_final)[:, N_META:]
    y_sample = rmsnorm(hs, norm_final)
    new_conv_prompt = jnp.stack(conv_p_list)
    new_ret_prompt = jnp.stack(ret_p_list)
    new_conv_sample = jnp.stack(conv_s_list)
    new_ret_sample = jnp.stack(ret_s_list)
    return (y_prompt, y_sample, new_conv_prompt, new_ret_prompt, new_conv_sample, new_ret_sample)


_drawn_inputs = setup_inputs


def setup_inputs(seed=0):
    import zlib

    import numpy as np

    out = dict(_drawn_inputs(seed))
    spreads = {}
    factors = {'norm_mlp': 3.573, 'norm_final': 2.859}
    for name, (base, spread) in spreads.items():
        noise = np.random.default_rng([zlib.crc32(name.encode()), seed]).standard_normal(out[name].shape)
        drawn = base * np.exp(spread * noise) if base else spread * noise
        out[name] = __import__('jax').numpy.asarray(drawn.astype(out[name].dtype))
    for name, factor in factors.items():
        out[name] = (out[name] * factor).astype(out[name].dtype)
    return out
```

```python
from contextlib import ExitStack

import concourse.bass as bass
import numpy as np
from concourse import mybir
from concourse.alu_op_type import AluOpType as ALU

F32 = mybir.dt.float32
F32R = mybir.dt.float32r
ACT = mybir.ActivationFunctionType

P = 128
D = 1024
META = 16
SEQ = 1024
SAMPLES = 8
PAST = 8192
HEADS = 4
DFF = 4 * D
EPS = 1e-6
DK = 128
KT = D // P
PROMPT = META + SEQ
COLS = PROMPT + SAMPLES
XT = -(-COLS // P)
LAST = COLS - (XT - 1) * P
TAIL = PROMPT - (XT - 1) * P
NT = 3
TW = (COLS - META) // NT
START = [META + TW * t for t in range(NT)]
MID = 4
BLOCKS = DFF // (MID * P)
INUNITS = 6
CH = D // 2
SCALE = float(DK) ** -0.5
U0, C0, B0, Q0, K0, V0, G0 = (4 * i for i in range(7))
GMIX, GMLP, CW, CACHE = 0, KT, 2 * KT, 2 * KT + 12
PROWS = CACHE + SAMPLES * 2 * 4
GAM, GAMP, GAMT, KDEC, KDECT = range(5)
G_IN = 2 * XT
G_HEAD = INUNITS * NT
G_OUT = G_IN + HEADS * G_HEAD
G_MLP = G_OUT + KT * NT
G_BLOCK = MID * NT + KT * NT
U_IN = 4
U_OUT = U_IN + HEADS * INUNITS
U_MLP = U_OUT + KT
LOADS_OUT = [1 + 2 * HEADS] * 3 + [1]
LOADS_MLP = [LOADS_OUT[0] + KT // 2, LOADS_OUT[1] + KT // 2, LOADS_OUT[2], LOADS_OUT[3]]


def wide(t):
    return (0, START[0] + TW) if t == 0 else (START[t], START[t] + TW)


def narrow(t):
    return START[t], START[t] + TW


def tok(i):
    return P * i, min(P * i + P, COLS)


def program(nc, io):
    ctx = ExitStack()
    with ctx:
        place = [16512]

        def at(name, shape, dt, offset):
            return nc.alloc_sbuf_tensor_at(name, [P, *shape], dt, offset=offset)

        def region(size):
            here = place[0]
            place[0] = here + -(-size // 32) * 32
            assert place[0] <= 229344, place[0]
            return here

        def sem(name):
            return ctx.enter_context(nc.semaphore(name))

        W4 = 4 * COLS
        a = region(2 * KT * W4)
        x_hi = at("x_hi", [KT, COLS], F32R, a)
        x_lo = at("x_lo", [KT, COLS], F32R, a + KT * W4)
        y = region(KT * W4)
        wv_hi = at("wv_hi", [KT, CH], F32R, y)
        wv_lo = at("wv_lo", [KT, CH], F32R, y + KT * CH * 4)
        y_raw = at("y_raw", [KT, COLS], F32, y)
        y_lo = at("y_lo", [KT, COLS], F32R, y)
        mid_hi = at("mid_hi", [MID, NT * TW], F32R, y)
        mid_lo = at("mid_lo", [MID, NT * TW], F32R, y + MID * NT * TW * 4)
        o = region(XT * CH * 4 + 4 * W4)
        v = at("v", [XT, CH], F32, o)
        k_rot = at("k_rot", [COLS], F32, o + XT * CH * 4)
        q_rot = at("q_rot", [COLS], F32, o + XT * CH * 4 + W4)
        cosr = at("cosr", [COLS], F32, o + XT * CH * 4 + 2 * W4)
        sinr = at("sinr", [COLS], F32, o + XT * CH * 4 + 3 * W4)
        y_hi = at("y_hi", [KT, COLS], F32R, o)
        acc = at("acc", [KT, COLS], F32, o)
        w = region(4 * 4096)
        w_raw = at("w_raw", [4, 1024], F32, w)
        w_hi = at("w_hi", [2, 1024], F32R, region(2 * 4096))
        w_lo = at("w_lo", [2, 1024], F32R, region(2 * 4096))
        rstd_b = at("rstd_b", [COLS], F32, region(W4))
        t = region(3 * W4 + XT * P * 4 + 2 * 4096)
        x_raw = at("x_raw", [3, D], F32, t)
        cu = at("cu", [COLS], F32, t)
        u_n = at("u_n", [COLS], F32, t + W4)
        o_tok = at("o_tok", [XT, P], F32, t + 2 * W4)
        q_dec = at("q_dec", [COLS], F32, t + 2 * W4 + XT * P * 4)
        state = at("state", [SAMPLES, P], F32, t + 3 * W4 + XT * P * 4)
        v_bc = at("v_bc", [SAMPLES, P], F32, t + 3 * W4 + XT * P * 4 + 4096)
        h_f32 = at("h_f32", [2, TW], F32, t)
        h_sq = at("h_sq", [2, TW], F32, t + 8 * TW)
        ssq_h = at("ssq_h", [NT * TW], F32, t + 16 * TW)
        gain_f = at("gain_f", [D], F32, t + 16 * TW + 4 * NT * TW)
        y_out = at("y_out", [2, D], F32, t + 16 * TW + 4 * NT * TW + 4096)
        r1, r2 = region(8 * (START[0] + TW)), region(8 * (START[0] + TW))
        rot1 = at("rot1", [2, START[0] + TW], F32, r1)
        rot2 = at("rot2", [2, START[0] + TW], F32, r2)
        diag = at("diag", [2, P], F32, r1)
        prm_raw = at("prm_raw", [P], F32, r2)
        c_rows = at("c_rows", [CH], F32, r1)
        k_tok = at("k_tok", [2, P], F32, w + 3 * 4096)
        s_msk = at("s_msk", [2, P], F32, w + 3 * 4096 + 1024)
        v_tail = at("v_tail", [P], F32, w + 3 * 4096 + 2048)
        S = at("S", [P], F32, region(512))
        mask = at("mask", [HEADS, P], F32, region(2048))
        dec = at("dec", [HEADS, P], F32, region(2048))
        hsc = at("hsc", [HEADS, 8], F32, region(128))
        ident = at("ident", [P], F32, region(512))
        ones = at("ones", [P], F32, region(512))
        prm = at("prm", [PROWS], F32, region(4 * PROWS))
        small = at("small", [104], F32, region(416))
        eps = small[:, 0:1]
        ssq_x, std_x, rstd_x = small[:, 1:10], small[:, 10:19], small[:, 19:28]
        ms_o, std_o, rstd_o = small[:, 28:37], small[:, 37:46], small[:, 46:55]
        k_smp, o_smp, sq_smp = small[:, 55:63], small[:, 63:71], small[:, 71:79]
        std_smp, rstd_smp = small[:, 79:87], small[:, 87:95]
        ssq_f, ms_f, std_f, rstd_f = small[:, 96:98], small[:, 98:100], small[:, 100:102], small[:, 102:104]
        c_tail = at("c_tail", [HEADS, 2 + SAMPLES], F32, region(160))

        bank = [ctx.enter_context(nc.psum_tensor(f"bank{i}", [P, 512], F32)) for i in range(8)]
        MAIN = bank[0:3]
        O_B, SC_B, KT_B, S_B, SMP_B = bank[3:8]
        XT_B = [(bank[3], bank[4]), (bank[5], bank[6])]

        x_in = [sem(f"x_in{i}") for i in range(3)]
        raw_in = [sem(f"raw_in{i}") for i in range(4)]
        ident_in, prm_in, tab_in, rope_in = sem("ident_in"), sem("prm_in"), sem("tab_in"), sem("rope_in")
        vs_out, state_in, vbc_in, gain_in = sem("vs_out"), sem("state_in"), sem("vbc_in"), sem("gain_in")
        state_out, S_out, conv_out = sem("state_out"), sem("S_out"), sem("conv_out")
        y_stored = [sem("y_stored0"), sem("y_stored1")]
        const_set, prm_t, prm_ready = sem("const_set"), sem("prm_t"), sem("prm_ready")
        xT_done, xhi_done, xlo_done = sem("xT_done"), sem("xhi_done"), sem("xlo_done")
        ssqx_done, stdx_done, rstdx_done, diag_done = sem("ssqx_done"), sem("stdx_done"), sem("rstdx_done"), sem("diag_done")
        rope_ready = sem("rope_ready")
        w_gained, w_high, w_ready = sem("w_gained"), sem("w_high"), sem("w_ready")
        main_done, main_read = sem("main_done"), sem("main_read")
        rot_added, q_ready, u_ready, gate_ready = sem("rot_added"), sem("q_ready"), sem("u_ready"), sem("gate_ready")
        conv_done = sem("conv_done")
        score_done, masked, ktok_ready = sem("score_done"), sem("masked"), sem("ktok_ready")
        o_done, o_read, Sinc_done, S_ready = sem("o_done"), sem("o_read"), sem("Sinc_done"), sem("S_ready")
        std_ready, o_normed, yT_done, y_ready = sem("std_ready"), sem("o_normed"), sem("yT_done"), sem("y_ready")
        ksmp_ready, state_dec, state_new = sem("ksmp_ready"), sem("state_dec"), sem("state_new")
        smp_done, smp_sq, smp_sum, smp_std = sem("smp_done"), sem("smp_sq"), sem("smp_sum"), sem("smp_std")
        silu_done, vtail_ready = sem("silu_done"), sem("vtail_ready")
        yhi_done, ylo_done = sem("yhi_done"), sem("ylo_done")
        ctail_done, ctailT_done, crows_ready = sem("ctail_done"), sem("ctailT_done"), sem("crows_ready")
        h_ready, hhi_done, hlo_done, hsq_done, ssq_done = sem("h_ready"), sem("hhi_done"), sem("hlo_done"), sem("hsq_done"), sem("ssq_done")
        sum_done, std2_done, rstd2_done = sem("sum_done"), sem("std2_done"), sem("rstd2_done")
        msq_done, mhi_done, mid_ready, acc_set = sem("msq_done"), sem("mhi_done"), sem("mid_ready"), sem("acc_set")
        fT_done, fsq_done, fms_done, fstd_done, frstd_done, f_ready = (sem(n) for n in (
            "fT_done", "fsq_done", "fms_done", "fstd_done", "frstd_done", "f_ready"))
        dve_own, passed = sem("dve_own"), sem("passed")

        def wait_alone(engine, semaphore, value):
            engine.wait_ge(semaphore, value)
            engine.sem_inc(passed, 1)

        w_in_t = io["w_in"][0].rearrange("(k p) n -> p k n", p=P)
        w_out_t = io["w_out"][0].rearrange("(k p) n -> p k n", p=P)
        w_up_t = io["w_up"][0].rearrange("(k p) n -> p k n", p=P)
        w_down_t = io["w_down"][0].rearrange("(k p) n -> p k n", p=P)
        xp, xs, meta = io["x_prompt"][0], io["x_sample"], io["meta_tokens"]
        IN_TILES = [K0, Q0, U0, C0, B0, G0]

        def raw_loaded_in(h, n):
            return 16 * (2 + n // 3) + 32 * h

        def raw_loaded_mlp(b, m):
            return 16 * (LOADS_MLP[m % 4] + m // 4 + 1) + 32 * b

        def unit(slot, ktiles):
            return w_raw[:, slot, :].rearrange("p (k n) -> p k n", k=ktiles)

        block = ctx.enter_context(nc.Block())

        @block.sync
        def _(sp):
            def load_x(i):
                if i >= 3:
                    sp.wait_ge(xlo_done, 2 * (i - 2))
                    sp.wait_ge(ssqx_done, i - 2)
                s = i % 3
                if i == 0:
                    sp.dma_start(x_raw[META:P, s, :], xp[0:P - META, :]).then_inc(x_in[s], 16)
                    sp.dma_start(x_raw[0:META, s, :], meta).then_inc(x_in[s], 16)
                elif i == XT - 1:
                    sp.dma_start(x_raw[0:TAIL, s, :], xp[SEQ - TAIL:SEQ, :]).then_inc(x_in[s], 16)
                    sp.dma_start(x_raw[TAIL:LAST, s, :], xs.rearrange("b s d -> (b s) d")).then_inc(x_in[s], 16)
                else:
                    sp.dma_start(x_raw[:, s, :], xp[P * i - META:P * i - META + P, :]).then_inc(x_in[s], 16)

            sp.dma_start(ident[:, :], io["ident"]).then_inc(ident_in, 16)
            load_x(0)
            sp.dma_start(prm_raw[GMIX:GMIX + KT, :], io["norm_mix"].rearrange("l (k p) -> (l k) p", p=P)).then_inc(prm_in, 16)
            sp.dma_start(prm_raw[GMLP:GMLP + KT, :], io["norm_mlp"].rearrange("l (k p) -> (l k) p", p=P)).then_inc(prm_in, 16)
            sp.dma_start(prm_raw[CW:CW + 12, :], io["conv_w"].rearrange("l r (c p) -> (l r c) p", p=P)).then_inc(prm_in, 16)
            sp.dma_start(prm_raw[CACHE:PROWS, :], io["cache_conv"].rearrange("l b r (c p) -> (l b r c) p", p=P)).then_inc(prm_in, 16)
            for u in range(U_IN):
                sp.dma_start(unit(u, 2), w_in_t[:, 2 * u:2 * u + 2, V0 * P:(V0 + 4) * P]).then_inc(raw_in[u], 16)
                if u < 2:
                    load_x(u + 1)
            for i in range(3, XT):
                load_x(i)
            sp.dma_start(cosr[:, :], io["cos_t"]).then_inc(rope_in, 16)
            sp.dma_start(sinr[:, :], io["sin_t"]).then_inc(rope_in, 16)
            sp.dma_start(mask[:, :, :], io["mask_t"]).then_inc(tab_in, 16)
            sp.dma_start(dec[:, :, :], io["dec_t"]).then_inc(tab_in, 16)
            sp.dma_start(hsc[:, :, :], io["hsc_t"]).then_inc(tab_in, 16)
            sp.dma_start(io["new_conv_sample"][0, :, 0, :], io["cache_conv"][0, :, 1, :]).then_inc(conv_out, 16)
            with sp.Fori(0, HEADS) as h:
                for n in range(INUNITS):
                    wait_alone(sp, w_ready, INUNITS * h + (U_IN + n - 2))
                    sp.dma_start(unit(n % 3, KT), w_in_t[:, :, bass.ds(h * P + IN_TILES[n] * P, P)]).then_inc(raw_in[n % 3], 16)
                    if n == 3:
                        wait_alone(sp, smp_done, h + 1)
                        wait_alone(sp, state_out, 16 * h + 16)
                        sp.wait_ge(vs_out, 16)
                        sp.dma_start(state[:, :, :], io["state_ret"][0, :, bass.ds(h, 1), :, :].rearrange("b h d e -> d (b h) e")).then_inc(state_in, 16)
                        sp.dma_start(v_bc[:, :, :], io["v_smp"][:, bass.ds(h * P, P)].unsqueeze(0).to_broadcast([P, SAMPLES, P])).then_inc(vbc_in, 16)
            with sp.Fori(0, KT // 2) as j:
                for n in range(2):
                    wait_alone(sp, w_ready, 2 * j + (U_OUT + n - 1))
                    sp.dma_start(unit(n, KT), w_out_t[:, :, bass.ds(j * 2 * P + n * P, P)]).then_inc(raw_in[n], 16)

            def load_mlp(b, m, split):
                wait_alone(sp, w_ready, split)
                if m < MID:
                    src = w_up_t[:, :, bass.ds(b * MID * P + m * P, P)]
                    sp.dma_start(unit(m % 4, KT), src).then_inc(raw_in[m % 4], 16)
                else:
                    src = w_down_t[:, bass.ds(b * MID, MID), 256 * (m - MID):256 * (m - MID) + 256]
                    sp.dma_start(unit(m % 4, MID), src).then_inc(raw_in[m % 4], 16)

            for m in range(8):
                load_mlp(0, m, U_MLP + m - 1 if m < 2 else U_MLP + m - 3)
            sp.wait_ge(rstd2_done, NT)
            sp.wait_ge(state_out, 16 * HEADS + 16)
            sp.dma_start(gain_f[:, :], io["norm_final"].unsqueeze(0).to_broadcast([P, D])).then_inc(gain_in, 16)
            with sp.Fori(1, BLOCKS) as b:
                for m in range(8):
                    load_mlp(b, m, 8 * b + (U_MLP + m - 3))
            for i in range(SEQ // P + 1):
                sp.wait_ge(f_ready, i + 1)
                if i < SEQ // P:
                    sp.dma_start(io["y_prompt"][0, P * i:P * i + P, :], y_out[:, i % 2, :]).then_inc(y_stored[i % 2], 16)
                else:
                    sp.dma_start(io["y_sample"].rearrange("b s d -> (b s) d"), y_out[0:SAMPLES, i % 2, :]).then_inc(y_stored[i % 2], 16)
            sp.wait_ge(y_stored[0], 16 * 5)
            sp.wait_ge(y_stored[1], 16 * 4)
            sp.wait_ge(conv_out, 48)
            sp.wait_ge(state_out, 16 * HEADS + 16)
            sp.wait_ge(S_out, 16 * HEADS + 16)

        @block.gpsimd
        def _(pool):
            g = nc.gpsimd

            def gain(slot, loaded, gtile, ktiles=KT, k0=0):
                pool.wait_ge(raw_in[slot], loaded)
                wt = unit(slot, ktiles)
                gb = prm[:, gtile + k0:gtile + k0 + ktiles].unsqueeze(2).to_broadcast([P, ktiles, 1024 // ktiles])
                g.tensor_tensor(wt, wt, gb, ALU.mult).then_inc(w_gained, 1)

            pool.wait_ge(prm_ready, 1)
            for u in range(U_IN):
                gain(u, 16, GMIX, 2, 2 * u)
            gain(0, raw_loaded_in(0, 0), GMIX)
            pool.wait_ge(rope_in, 32)
            pool.wait_ge(main_read, G_IN)
            g.tensor_tensor(cosr[:, :], cosr[:, :], rstd_b[:, :], ALU.mult)
            g.tensor_tensor(sinr[:, :], sinr[:, :], rstd_b[:, :], ALU.mult).then_inc(rope_ready, 1)

            def head(h, last):
                for n in range(INUNITS):
                    if n + 1 < INUNITS:
                        gain((n + 1) % 3, raw_loaded_in(h, n + 1), GMIX)
                    elif not last:
                        gain(0, raw_loaded_in(h + 1, 0), GMIX)
                    if n < 2:
                        for t in range(NT):
                            pool.wait_ge(main_read, G_HEAD * h + (G_IN + NT * n + t + 1))
                            a0, a1 = wide(t)
                            s = (NT * n + t) % 2
                            dst = (k_rot, q_rot)[n]
                            g.tensor_tensor(dst[:, a0:a1], rot1[:, s, 0:a1 - a0], rot2[:, s, 0:a1 - a0], ALU.add).then_inc(rot_added, 1)
                    if n == 1:
                        pool.wait_ge(rot_added, 6 * h + 6)
                        pool.wait_ge(tab_in, 48)
                        full = (XT - 1) * P
                        g.tensor_tensor(q_dec[:, 0:full].rearrange("p (c i) -> p c i", i=P),
                                        q_rot[:, 0:full].rearrange("p (c i) -> p c i", i=P),
                                        dec[:, bass.ds(h, 1), :].to_broadcast([P, XT - 1, P]), ALU.mult)
                        g.tensor_tensor(q_dec[:, full:full + TAIL].unsqueeze(1), q_rot[:, full:full + TAIL].unsqueeze(1),
                                        dec[:, bass.ds(h, 1), 0:TAIL], ALU.mult).then_inc(q_ready, 1)
                    if n == 2:
                        for t in range(NT):
                            pool.wait_ge(main_read, G_HEAD * h + (G_IN + NT * n + t + 1))
                            a0, a1 = wide(t)
                            g.tensor_tensor(u_n[:, a0:a1], u_n[:, a0:a1], rstd_b[:, a0:a1], ALU.mult).then_inc(u_ready, 1)
                    if n == 3:
                        pool.wait_ge(conv_done, h + 1)
                        yc = y_raw[:, bass.ds(h, 1), META:COLS]
                        g.tensor_tensor(yc, yc, rstd_b[:, META:COLS].unsqueeze(1), ALU.mult).then_inc(gate_ready, 1)

            with pool.Fori(0, HEADS - 1) as h:
                head(h, False)
            head(HEADS - 1, True)

            pool.wait_ge(y_ready, 4 * HEADS + 4)
            g.memset(ssq_h[:, :], 0.0).then_inc(ssq_done, 1)

            def squares(j, last):
                for i in range(2 * NT):
                    if last and i == NT:
                        gain(0, raw_loaded_mlp(0, 0), GMLP)
                    pool.wait_ge(hsq_done, 6 * j + i + 1)
                    pool.wait_ge(ssq_done, 6 * j + i + 1)
                    c0 = (i % NT) * TW
                    g.tensor_tensor(ssq_h[:, c0:c0 + TW], ssq_h[:, c0:c0 + TW], h_sq[:, i % 2, :], ALU.add).then_inc(ssq_done, 1)
            with pool.Fori(0, KT // 2 - 1) as j:
                squares(j, False)
            squares(KT // 2 - 1, True)
            gain(1, raw_loaded_mlp(0, 1), GMLP)
            pool.wait_ge(main_done, G_MLP)
            pool.wait_ge(hlo_done, KT * NT)
            for n in range(KT):
                if n == 2 or n == 5:
                    gain(2 + n // 5, raw_loaded_mlp(0, 2 + n // 5), GMLP)
                g.tensor_tensor(acc[:, n, META:COLS], x_hi[:, n, META:COLS], x_lo[:, n, META:COLS], ALU.add).then_inc(acc_set, 1)
            with pool.Fori(1, BLOCKS) as b:
                for m in range(MID):
                    gain(m, raw_loaded_mlp(b, m), GMLP)

        @block.scalar
        def _(act):
            s = nc.scalar

            def high(slot, dst_slot, used):
                if used is not None:
                    act.wait_ge(main_done, used)
                s.activation(w_hi[:, dst_slot, :], w_raw[:, slot, :], ACT.Copy).then_inc(w_high, 1)

            act.sem_inc(state_out, 16)
            act.sem_inc(S_out, 16)
            act.sem_inc(smp_std, 1)
            act.wait_ge(prm_t, 1)
            s.activation(prm[:, :], SMP_B[:, 0:PROWS], ACT.Copy).then_inc(prm_ready, 1)
            for i in range(XT):
                c0, c1 = tok(i)
                rows = c1 - c0
                for hf in range(2):
                    act.wait_ge(xT_done, 2 * i + hf + 1)
                    src = XT_B[i % 2][hf][:, :].rearrange("p (k c) -> p k c", c=P)[:, :, 0:rows]
                    s.activation(x_hi[:, 4 * hf:4 * hf + 4, c0:c1], src, ACT.Copy).then_inc(xhi_done, 1)
                if i == 0:
                    for u in range(U_IN):
                        act.wait_ge(w_gained, u + 1)
                        s.activation(wv_hi[:, 2 * u:2 * u + 2, :], unit(u, 2), ACT.Copy).then_inc(w_high, 1)
                act.wait_ge(x_in[i % 3], 16 * (i // 3 + 1) + 16 * (i % 3 == 0) + 16 * (i == XT - 1))
                s.activation(q_dec[0:rows, 0:D], x_raw[0:rows, i % 3, :], ACT.Square, accum_out=ssq_x[0:rows, i:i + 1]).then_inc(ssqx_done, 1)
                act.wait_ge(ssqx_done, i + 1)
                if i == 0:
                    act.wait_ge(const_set, 2)
                s.activation(std_x[0:rows, i:i + 1], ssq_x[0:rows, i:i + 1], ACT.Sqrt, scale=1.0 / D, bias=eps[0:rows, :]).then_inc(stdx_done, 1)
            act.wait_ge(w_gained, U_IN + 1)
            high(0, 0, None)
            act.wait_ge(main_read, G_IN - 2)
            act.dma_start(io["v_smp"], v[TAIL:LAST, XT - 1, :]).then_inc(vs_out, 16)

            def head(h, last):
                for n in range(INUNITS):
                    if n + 1 < INUNITS or not last:
                        act.wait_ge(w_gained, INUNITS * h + (U_IN + n + 2))
                    else:
                        act.wait_ge(raw_in[0], 16 * (LOADS_OUT[0] + 1))
                    high((n + 1) % 3 if n + 1 < INUNITS else 0, (n + 1) % 2, G_HEAD * h + (G_IN + NT * n))
                    for t in range(NT):
                        j = NT * n + t
                        if j == 4:
                            wait_alone(act, rot_added, 6 * h + 3)
                            s.activation(k_smp, k_rot[:, PROMPT:COLS], ACT.Copy, scale=SCALE).then_inc(ksmp_ready, 1)
                            s.activation(v_tail[0:TAIL, :].unsqueeze(1), v[0:TAIL, XT - 1:XT, bass.ds(h * P, P)], ACT.Copy).then_inc(vtail_ready, 1)
                        if 8 <= j <= 16:
                            c = j - 8
                            rows = P if c < XT - 1 else TAIL
                            act.wait_ge(o_done, 9 * h + c + 1)
                            s.activation(o_tok[0:rows, c, :], O_B[0:rows, 0:P], ACT.Copy)
                            s.activation(O_B[0:rows, P:2 * P], O_B[0:rows, 0:P], ACT.Square, accum_out=ms_o[0:rows, c:c + 1]).then_inc(o_read, 1)
                            act.wait_ge(o_read, 9 * h + c + 1)
                        if 7 <= j <= 15:
                            c = j - 7
                            rows = P if c < XT - 1 else TAIL
                            kd = KDEC if c < XT - 1 else KDECT
                            wait_alone(act, score_done, 9 * h + c + 1)
                            s.activation(k_tok[0:rows, c % 2, :], KT_B[0:rows, 0:P], ACT.Copy,
                                         scale=hsc[0:rows, bass.ds(h, 1), kd:kd + 1].rearrange("p a b -> p (a b)")).then_inc(ktok_ready, 1)
                        if j == 12:
                            wait_alone(act, state_in, 16 * h + 16)
                            s.activation(state[:, :, :], state[:, :, :], ACT.Copy,
                                         scale=hsc[:, bass.ds(h, 1), GAM:GAM + 1].rearrange("p a b -> p (a b)")).then_inc(state_dec, 1)
                        if j == 14:
                            act.wait_ge(state_new, h + 1)
                            act.dma_start(io["new_ret_sample"][0, :, bass.ds(h, 1), :, :].rearrange("b h d e -> d (b h) e"), state[:, :, :]).then_inc(state_out, 16)
                        if j == 16:
                            s.activation(std_o[:, 0:XT - 1], ms_o[:, 0:XT - 1], ACT.Sqrt, scale=1.0 / DK, bias=eps)
                            s.activation(std_o[0:TAIL, XT - 1:XT], ms_o[0:TAIL, XT - 1:XT], ACT.Sqrt, scale=1.0 / DK, bias=eps[0:TAIL, :]).then_inc(std_ready, 1)
                            act.wait_ge(S_ready, 9 * h + 9)
                            act.dma_start(io["new_ret_prompt"][0, 0, bass.ds(h, 1), :, :].rearrange("h d e -> (h d) e"), S[:, :]).then_inc(S_out, 16)
                            act.wait_ge(smp_done, h + 2)
                            s.activation(o_smp, SMP_B[:, 0:SAMPLES], ACT.Copy)
                            s.activation(sq_smp, SMP_B[:, 0:SAMPLES], ACT.Square).then_inc(smp_sq, 1)
                if last:
                    c0, c1 = narrow(0)
                    act.wait_ge(main_read, G_HEAD * h + (G_IN + 5 * NT))
                    act.wait_ge(y_ready, 4 * h + 4)
                    s.activation(y_hi[:, 0:KT - 1, c0:c1], y_raw[:, 0:KT - 1, c0:c1], ACT.Copy).then_inc(yhi_done, 1)
                act.wait_ge(smp_sum, h + 1)
                s.activation(std_smp, SMP_B[:, 16:16 + SAMPLES], ACT.Sqrt, scale=1.0 / DK, bias=eps).then_inc(smp_std, 1)
                for t in range(NT):
                    a0, a1 = narrow(t)
                    wait_alone(act, main_read, G_HEAD * h + (G_IN + NT * 5 + t + 1))
                    yg = y_raw[:, bass.ds(4 + h, 1), a0:a1]
                    s.activation(yg, yg, ACT.Silu).then_inc(silu_done, 1)

            with act.Fori(0, HEADS - 1) as h:
                head(h, False)
            head(HEADS - 1, True)

            c0, c1 = narrow(0)
            act.wait_ge(y_ready, 4 * HEADS + 1)
            s.activation(y_hi[:, KT - 1, c0:c1], y_raw[:, KT - 1, c0:c1], ACT.Copy).then_inc(yhi_done, 1)
            for t in range(1, NT):
                a0, a1 = narrow(t)
                act.wait_ge(y_ready, 4 * HEADS + (2 if t == 1 else 4))
                s.activation(y_hi[:, :, a0:a1], y_raw[:, :, a0:a1], ACT.Copy).then_inc(yhi_done, 1)
            act.wait_ge(ctailT_done, 1)
            s.activation(c_rows[0:2 + SAMPLES, :], SMP_B[0:2 + SAMPLES, :], ACT.Copy).then_inc(crows_ready, 1)
            act.wait_ge(crows_ready, 1)
            act.dma_start(io["new_conv_prompt"][0, 0, :, :], c_rows[0:2, :]).then_inc(conv_out, 16)
            act.dma_start(io["new_conv_sample"][0, :, 1, :], c_rows[2:2 + SAMPLES, :]).then_inc(conv_out, 16)

            def out_pair(j, last):
                for n in range(2):
                    if n == 0:
                        act.wait_ge(raw_in[1], 16 * j + 16 * (LOADS_OUT[1] + 1))
                        high(1, 1, 6 * j + G_OUT)
                    elif not last:
                        act.wait_ge(raw_in[0], 16 * j + 16 * (LOADS_OUT[0] + 2))
                        high(0, 0, 6 * j + (G_OUT + NT))
                    else:
                        act.wait_ge(w_gained, U_OUT + 1)
                        high(0, 0, 6 * j + (G_OUT + NT))
                    for t in range(NT):
                        i = NT * n + t
                        a0, a1 = narrow(t)
                        wait_alone(act, h_ready, 6 * j + i + 1)
                        s.activation(x_hi[:, bass.ds(2 * j + n, 1), a0:a1], h_f32[:, i % 2, :].unsqueeze(1), ACT.Copy).then_inc(hhi_done, 1)
                        if i >= 2:
                            act.wait_ge(ssq_done, 6 * j + i)
                        else:
                            act.wait_ge(ssq_done, 6 * j + 1)
                        s.activation(h_sq[:, i % 2, :], h_f32[:, i % 2, :], ACT.Square).then_inc(hsq_done, 1)

            with act.Fori(0, KT // 2 - 1) as j:
                out_pair(j, False)
            out_pair(KT // 2 - 1, True)
            for t in range(NT):
                c0 = META + t * TW
                act.wait_ge(sum_done, t + 1)
                s.activation(rstd_b[:, c0:c0 + TW], (O_B, SC_B, KT_B)[t][:, 0:TW], ACT.Sqrt, scale=1.0 / D, bias=eps).then_inc(std2_done, 1)

            def mlp(b, last):
                for m in range(8):
                    if m + 1 < 8 or not last:
                        nxt = (m + 1) % 8
                        if nxt < MID and nxt:
                            act.wait_ge(w_gained, 4 * b + (U_OUT + nxt + 1))
                        elif nxt:
                            act.wait_ge(raw_in[nxt % 4], raw_loaded_mlp(b, nxt))
                        else:
                            act.wait_ge(w_gained, 4 * b + (U_OUT + 4 + 1))
                        high(nxt % 4, nxt % 2, G_BLOCK * b + (G_MLP + (NT * m if m < MID else NT * MID + 2 * NT * (m - MID))))
                    if m < MID:
                        for t in range(NT):
                            i = NT * m + t
                            act.wait_ge(main_read, G_BLOCK * b + (G_MLP + i + 1))
                            s.activation(h_sq[:, i % 2, :], h_f32[:, i % 2, :], ACT.Square).then_inc(msq_done, 1)
                            act.wait_ge(msq_done, 12 * b + i + 1)
                            s.activation(mid_hi[:, m, t * TW:(t + 1) * TW], h_sq[:, i % 2, :], ACT.Copy).then_inc(mhi_done, 1)

            with act.Fori(0, BLOCKS - 1) as b:
                mlp(b, False)
            mlp(BLOCKS - 1, True)

            for i in range(SEQ // P + 1):
                rows = P if i < SEQ // P else SAMPLES
                for hf in range(2):
                    act.wait_ge(fT_done, 2 * i + hf + 1)
                    if i:
                        act.wait_ge(fms_done, i)
                    s.activation(h_f32[0:rows, :, :].rearrange("p a b -> p (a b)")[:, 0:512], XT_B[i % 2][hf][0:rows, :], ACT.Square, accum_out=ssq_f[0:rows, hf:hf + 1]).then_inc(fsq_done, 1)
                    act.wait_ge(fsq_done, 2 * i + hf + 1)
                act.wait_ge(fms_done, i + 1)
                s.activation(std_f[0:rows, 0:1], ms_f[0:rows, 0:1], ACT.Sqrt, scale=1.0 / D, bias=eps[0:rows, :]).then_inc(fstd_done, 1)

        @block.vector
        def _(dve):
            d = nc.vector

            def low(slot, dst_slot, high_count):
                dve.wait_ge(w_high, high_count)
                d.tensor_tensor(w_lo[:, dst_slot, :], w_raw[:, slot, :], w_hi[:, dst_slot, :], ALU.subtract).then_inc(w_ready, 1)

            dve.sem_inc(y_ready, 4)
            d.memset(eps, EPS).then_inc(const_set, 1)
            d.memset(ones[:, :], 1.0).then_inc(const_set, 1)

            def read_v(i):
                rows = tok(i)[1] - tok(i)[0]
                gi = max(2 * i - 1, 0)
                dve.wait_ge(main_done, gi + 1)
                d.tensor_scalar(v[0:rows, i, :], MAIN[gi % 3][0:rows, :], rstd_x[0:rows, i:i + 1], None, ALU.mult).then_inc(main_read, 1)

            def read_r(i):
                c0, c1 = tok(i)
                gi = 2 * i + 2 if i < XT - 1 else 2 * i + 1
                dve.wait_ge(main_done, gi + 1)
                d.tensor_copy(rstd_b[:, c0:c1], MAIN[gi % 3][:, 0:c1 - c0]).then_inc(main_read, 1)

            def row_rms(i):
                rows = tok(i)[1] - tok(i)[0]
                dve.wait_ge(stdx_done, i + 1)
                d.reciprocal(rstd_x[0:rows, i:i + 1], std_x[0:rows, i:i + 1]).then_inc(rstdx_done, 1)
                dve.wait_ge(rstdx_done, i + 1)
                d.tensor_scalar(diag[0:rows, i % 2, 0:rows], ident[0:rows, 0:rows], rstd_x[0:rows, i:i + 1], None, ALU.mult).then_inc(diag_done, 1)

            dve.wait_ge(ident_in, 16)
            for i in range(XT):
                c0, c1 = tok(i)
                for hf in range(2):
                    dve.wait_ge(xhi_done, 2 * i + hf + 1)
                    src = XT_B[i % 2][hf][:, :].rearrange("p (k c) -> p k c", c=P)[:, :, 0:c1 - c0]
                    d.tensor_tensor(x_lo[:, 4 * hf:4 * hf + 4, c0:c1], src, x_hi[:, 4 * hf:4 * hf + 4, c0:c1], ALU.subtract).then_inc(xlo_done, 1)
                if i == 0:
                    for u in range(U_IN):
                        dve.wait_ge(w_high, u + 1)
                        d.tensor_tensor(wv_lo[:, 2 * u:2 * u + 2, :], unit(u, 2), wv_hi[:, 2 * u:2 * u + 2, :], ALU.subtract).then_inc(w_ready, 1)
                if i >= 2:
                    read_v(i - 2)
                if i >= 3:
                    read_r(i - 3)
                if i >= 1:
                    row_rms(i - 1)
            read_v(XT - 2)
            read_r(XT - 3)
            row_rms(XT - 1)
            low(0, 0, U_IN + 1)
            read_v(XT - 1)
            read_r(XT - 2)
            read_r(XT - 1)
            dve.wait_ge(rope_ready, 1)
            OWN = 5

            def head(h, last):
                own = [0]

                def mine(ins):
                    own[0] += 1
                    ins.then_inc(dve_own, 1)
                    dve.wait_ge(dve_own, OWN * h + own[0])

                for n in range(INUNITS):
                    low((n + 1) % 3 if n + 1 < INUNITS else 0, (n + 1) % 2, INUNITS * h + (U_IN + n + 2))
                    for t in range(NT):
                        j = NT * n + t
                        gi = G_HEAD * h + (G_IN + j)
                        pb = MAIN[t]
                        if j == 17:
                            dve.wait_ge(std_ready, h + 1)
                            d.reciprocal(rstd_o[:, 0:XT - 1], std_o[:, 0:XT - 1])
                            mine(d.reciprocal(rstd_o[0:TAIL, XT - 1:XT], std_o[0:TAIL, XT - 1:XT]))
                            d.tensor_tensor(o_tok[:, 0:XT - 1, :], o_tok[:, 0:XT - 1, :], rstd_o[:, 0:XT - 1].unsqueeze(2).to_broadcast([P, XT - 1, P]), ALU.mult)
                            d.tensor_scalar(o_tok[0:TAIL, XT - 1, :], o_tok[0:TAIL, XT - 1, :], rstd_o[0:TAIL, XT - 1:XT], None, ALU.mult).then_inc(o_normed, 1)
                            if last:
                                c0, c1 = narrow(0)
                                dve.wait_ge(yhi_done, 1)
                                d.tensor_tensor(y_lo[:, 0:KT - 1, c0:c1], y_raw[:, 0:KT - 1, c0:c1], y_hi[:, 0:KT - 1, c0:c1], ALU.subtract).then_inc(ylo_done, 1)
                        dve.wait_ge(main_done, gi + 1)
                        if n < 2:
                            a0, a1 = wide(t)
                            w = a1 - a0
                            sl = j % 2
                            if j >= 2:
                                dve.wait_ge(rot_added, 6 * h + (j - 1))
                            d.tensor_tensor(rot1[:, sl, 0:w], pb[:, 0:w], cosr[:, a0:a1], ALU.mult)
                            d.tensor_tensor(rot2[0:64, sl, 0:w], pb[64:128, 0:w], sinr[64:128, a0:a1], ALU.mult)
                            d.tensor_tensor(rot2[64:128, sl, 0:w], pb[0:64, 0:w], sinr[0:64, a0:a1], ALU.mult).then_inc(main_read, 1)
                        elif n == 2:
                            a0, a1 = wide(t)
                            d.tensor_tensor(u_n[:, a0:a1], pb[:, 0:a1 - a0], rstd_b[:, a0:a1], ALU.mult).then_inc(main_read, 1)
                        elif n == 3:
                            a0, a1 = wide(t)
                            dve.wait_ge(u_ready, 3 * h + t + 1)
                            d.tensor_tensor(cu[:, a0:a1], pb[:, 0:a1 - a0], u_n[:, a0:a1], ALU.mult).then_inc(main_read, 1)
                        elif n == 4:
                            a0, a1 = narrow(t)
                            if t == 0:
                                dve.wait_ge(gate_ready, h + 1)
                            yb = y_raw[:, bass.ds(h, 1), a0:a1]
                            d.tensor_tensor(yb, pb[:, 0:TW].unsqueeze(1), yb, ALU.mult).then_inc(main_read, 1)
                        else:
                            a0, a1 = narrow(t)
                            d.tensor_tensor(y_raw[:, bass.ds(4 + h, 1), a0:a1], pb[:, 0:TW].unsqueeze(1), rstd_b[:, a0:a1].unsqueeze(1), ALU.mult).then_inc(main_read, 1)
                        if 8 <= j <= 16:
                            c = j - 8
                            gp = GAMP if c < XT - 1 else GAMT
                            dve.wait_ge(Sinc_done, 9 * h + c + 1)
                            if c == 0:
                                dve.wait_ge(S_out, 16 * h + 16)
                                d.tensor_copy(S[:, :], S_B[:, 0:P]).then_inc(S_ready, 1)
                            else:
                                dve.wait_ge(S_ready, 9 * h + c)
                                d.scalar_tensor_tensor(out=S[:, :], in0=S[:, :], scalar=hsc[:, bass.ds(h, 1), gp:gp + 1].rearrange("p a b -> p (a b)"),
                                                       in1=S_B[:, 0:P], op0=ALU.mult, op1=ALU.add).then_inc(S_ready, 1)
                        if 7 <= j <= 15:
                            c = j - 7
                            rows = P if c < XT - 1 else TAIL
                            dve.wait_ge(score_done, 9 * h + c + 1)
                            d.tensor_tensor(s_msk[0:rows, c % 2, 0:rows].unsqueeze(1), SC_B[0:rows, 0:rows].unsqueeze(1), mask[0:rows, bass.ds(h, 1), 0:rows], ALU.mult).then_inc(masked, 1)
                        if j == 11:
                            def cw(r):
                                return prm[:, bass.ds(h + (CW + 4 * r), 1)]

                            def cache(r):
                                rows_ = prm[:, CACHE:PROWS].rearrange("p (b r c) -> p r c b", b=SAMPLES, r=2)
                                return rows_[:, r, bass.ds(h, 1), :]
                            dve.wait_ge(main_read, gi + 1)
                            yp = y_raw[:, bass.ds(h, 1), META:PROMPT]
                            ys = y_raw[:, bass.ds(h, 1), PROMPT:COLS]

                            def cucols(a0, a1):
                                return cu[:, a0:a1].unsqueeze(1)
                            d.tensor_scalar(yp, cucols(META - 2, PROMPT - 2), cw(0), None, ALU.mult)
                            mine(d.tensor_scalar(ys, cache(0), cw(0), None, ALU.mult))
                            d.scalar_tensor_tensor(out=yp, in0=cucols(META - 1, PROMPT - 1), scalar=cw(1), in1=yp, op0=ALU.mult, op1=ALU.add)
                            mine(d.scalar_tensor_tensor(out=ys, in0=cache(1), scalar=cw(1), in1=ys, op0=ALU.mult, op1=ALU.add))
                            d.tensor_copy(c_tail[:, bass.ds(h, 1), :], cucols(PROMPT - 2, COLS)).then_inc(ctail_done, 1)
                            d.scalar_tensor_tensor(out=yp, in0=cucols(META, PROMPT), scalar=cw(2), in1=yp, op0=ALU.mult, op1=ALU.add)
                            d.scalar_tensor_tensor(out=ys, in0=cucols(PROMPT, COLS), scalar=cw(2), in1=ys, op0=ALU.mult, op1=ALU.add).then_inc(conv_done, 1)
                        if j == 13:
                            dve.wait_ge(state_dec, h + 1)
                            dve.wait_ge(vbc_in, 16 * h + 16)
                            dve.wait_ge(ksmp_ready, h + 1)
                            for b in range(SAMPLES):
                                last_b = d.scalar_tensor_tensor(out=state[:, b, :], in0=v_bc[:, b, :], scalar=k_smp[:, b:b + 1], in1=state[:, b, :], op0=ALU.mult, op1=ALU.add)
                            last_b.then_inc(state_new, 1)
                full = (XT - 1) * P
                dve.wait_ge(silu_done, 3 * h + 3)
                for i, (a0, a1, pb, p0) in enumerate(((META, 512, SC_B, META), (512, full, KT_B, 0), (full, PROMPT, S_B, 0))):
                    dve.wait_ge(yT_done, 3 * h + i + 1)
                    yr = y_raw[:, bass.ds(4 + h, 1), a0:a1]
                    d.tensor_tensor(yr, pb[:, p0:p0 + a1 - a0].unsqueeze(1), yr, ALU.mult).then_inc(y_ready, 1)
                dve.wait_ge(smp_std, h + 2)
                mine(d.reciprocal(rstd_smp, std_smp))
                mine(d.tensor_tensor(rstd_smp, rstd_smp, o_smp, ALU.mult))
                yr = y_raw[:, bass.ds(4 + h, 1), PROMPT:COLS]
                d.tensor_tensor(yr, rstd_smp.unsqueeze(1), yr, ALU.mult).then_inc(y_ready, 1)
                assert own[0] == OWN

            with dve.Fori(0, HEADS - 1) as h:
                head(h, False)
            head(HEADS - 1, True)

            def y_low(tiles, t, count, dve=dve):
                a0, a1 = narrow(t)
                dve.wait_ge(yhi_done, count)
                d.tensor_tensor(y_lo[:, tiles, a0:a1], y_raw[:, tiles, a0:a1], y_hi[:, tiles, a0:a1], ALU.subtract).then_inc(ylo_done, 1)

            y_low(slice(KT - 1, KT), 0, 2)
            y_low(slice(0, KT), 1, 3)
            y_low(slice(0, KT), 2, 4)

            def out_pair(j, last):
                for n in range(2):
                    low((n + 1) % 2, (n + 1) % 2, 2 * j + (U_OUT + n + 2))
                    for t in range(NT):
                        i = NT * n + t
                        a0, a1 = narrow(t)
                        xh = x_hi[:, bass.ds(2 * j + n, 1), a0:a1]
                        xl = x_lo[:, bass.ds(2 * j + n, 1), a0:a1]
                        hb = h_f32[:, i % 2, :].unsqueeze(1)
                        dve.wait_ge(main_done, 6 * j + (G_OUT + i + 1))
                        if i >= 2:
                            dve.wait_ge(hsq_done, 6 * j + (i - 1))
                        else:
                            dve.wait_ge(ssq_done, 6 * j + 1)
                        d.tensor_tensor(hb, MAIN[t][:, 0:TW].unsqueeze(1), xh, ALU.add).then_inc(main_read, 1)
                        dve.wait_ge(main_read, 6 * j + (G_OUT + i + 1))
                        d.tensor_tensor(hb, hb, xl, ALU.add).then_inc(h_ready, 1)
                        dve.wait_ge(hhi_done, 6 * j + i + 1)
                        d.tensor_tensor(xl, hb, xh, ALU.subtract).then_inc(hlo_done, 1)

            with dve.Fori(0, KT // 2 - 1) as j:
                out_pair(j, False)
            out_pair(KT // 2 - 1, True)
            for t in range(NT):
                c0 = META + t * TW
                dve.wait_ge(std2_done, t + 1)
                d.reciprocal(rstd_b[:, c0:c0 + TW], rstd_b[:, c0:c0 + TW]).then_inc(rstd2_done, 1)
            dve.wait_ge(rstd2_done, NT)

            def mlp(b, last):
                for m in range(8):
                    if m + 1 < 8 or not last:
                        low((m + 1) % 4, (m + 1) % 2, 8 * b + (U_MLP + m + 2))
                    if m < MID:
                        for t in range(NT):
                            i = NT * m + t
                            a0, a1 = narrow(t)
                            dve.wait_ge(main_done, G_BLOCK * b + (G_MLP + i + 1))
                            d.scalar_tensor_tensor(out=h_f32[:, i % 2, :], in0=MAIN[t][:, 0:TW], scalar=0.0, in1=rstd_b[:, a0:a1],
                                                   op0=ALU.max, op1=ALU.mult).then_inc(main_read, 1)
                            dve.wait_ge(mhi_done, 12 * b + i + 1)
                            d.tensor_tensor(mid_lo[:, m, t * TW:(t + 1) * TW], h_sq[:, i % 2, :], mid_hi[:, m, t * TW:(t + 1) * TW], ALU.subtract).then_inc(mid_ready, 1)
                    else:
                        if m == MID:
                            dve.wait_ge(acc_set, KT)
                        for nn in range(2):
                            for t in range(NT):
                                a0, a1 = narrow(t)
                                n = 2 * (m - MID) + nn
                                dve.wait_ge(main_done, G_BLOCK * b + (G_MLP + NT * MID + NT * n + t + 1))
                                d.tensor_tensor(acc[:, n, a0:a1], MAIN[t][:, 0:TW], acc[:, n, a0:a1], ALU.add).then_inc(main_read, 1)

            with dve.Fori(0, BLOCKS - 1) as b:
                mlp(b, False)
            mlp(BLOCKS - 1, True)
            dve.wait_ge(gain_in, 16)
            for i in range(SEQ // P + 1):
                rows = P if i < SEQ // P else SAMPLES
                dve.wait_ge(fsq_done, 2 * i + 2)
                if i:
                    dve.wait_ge(fstd_done, i)
                d.tensor_tensor(ms_f[0:rows, 0:1], ssq_f[0:rows, 0:1], ssq_f[0:rows, 1:2], ALU.add).then_inc(fms_done, 1)
                dve.wait_ge(fstd_done, i + 1)
                d.reciprocal(rstd_f[0:rows, 0:1], std_f[0:rows, 0:1]).then_inc(frstd_done, 1)
                dve.wait_ge(frstd_done, i + 1)
                if i >= 2:
                    dve.wait_ge(y_stored[i % 2], 16 * (i // 2))
                for hf in range(2):
                    ins = d.scalar_tensor_tensor(out=y_out[0:rows, i % 2, 512 * hf:512 * hf + 512], in0=XT_B[i % 2][hf][0:rows, :],
                                                 scalar=rstd_f[0:rows, 0:1], in1=gain_f[0:rows, 512 * hf:512 * hf + 512], op0=ALU.mult, op1=ALU.mult)
                ins.then_inc(f_ready, 1)

        @block.tensor
        def _(pe):
            m_ = nc.tensor

            def three(out, pairs, waits=None):
                for i, (sh, sl, mh, ml) in enumerate(pairs):
                    if waits and i in waits:
                        pe.wait_ge(*waits[i])
                    m_.matmul(out, sh, mh, start=i == 0, stop=False)
                    m_.matmul(out, sh, ml, start=False, stop=False)
                    ins = m_.matmul(out, sl, mh, start=False, stop=i == len(pairs) - 1)
                return ins

            def transposes(i):
                c0, c1 = tok(i)
                rows = c1 - c0
                pe.wait_ge(x_in[i % 3], 16 * (i // 3 + 1) + 16 * (i % 3 == 0) + 16 * (i == XT - 1))
                if i >= 2:
                    pe.wait_ge(xlo_done, 2 * i - 2)
                for k in range(KT):
                    ins = m_.transpose(XT_B[i % 2][k // 4][:, P * (k % 4):P * (k % 4) + rows], x_raw[0:rows, i % 3, P * k:P * k + P], ident[0:rows, 0:rows])
                    if k % 4 == 3:
                        ins.then_inc(xT_done, 1)

            def v_rows(i):
                c0, c1 = tok(i)
                gi = max(2 * i - 1, 0)
                pe.wait_ge(xlo_done, 2 * i + 2)
                if gi >= 3:
                    pe.wait_ge(main_read, gi - 2)
                out = MAIN[gi % 3][0:c1 - c0, :]
                for k in range(KT):
                    if i == 0 and k % 2 == 0:
                        pe.wait_ge(w_ready, k // 2 + 1)
                    m_.matmul(out, x_hi[:, k, c0:c1], wv_hi[:, k, :], start=k == 0, stop=False)
                    m_.matmul(out, x_lo[:, k, c0:c1], wv_hi[:, k, :], start=False, stop=False)
                    if k < KT - 1:
                        m_.matmul(out, x_hi[:, k, c0:c1], wv_lo[:, k, :], start=False, stop=False)
                m_.matmul(out, x_hi[:, KT - 1, c0:c1], wv_lo[:, KT - 1, :], start=False, stop=True).then_inc(main_done, 1)

            def rms_columns(i):
                c0, c1 = tok(i)
                rows = c1 - c0
                gi = 2 * i + 2 if i < XT - 1 else 2 * i + 1
                pe.wait_ge(diag_done, i + 1)
                pe.wait_ge(main_read, gi - 2)
                m_.matmul(MAIN[gi % 3][:, 0:rows], ones[0:rows, :], diag[0:rows, i % 2, 0:rows], start=True, stop=True).then_inc(main_done, 1)

            pe.sem_inc(smp_done, 1)
            pe.wait_ge(ident_in, 16)
            pe.wait_ge(prm_in, 64)
            m_.transpose(SMP_B[:, 0:PROWS], prm_raw[0:PROWS, :], ident[0:PROWS, 0:PROWS]).then_inc(prm_t, 1)
            pe.wait_ge(const_set, 2)
            transposes(0)
            transposes(1)
            for i in range(XT):
                v_rows(i)
                if i + 2 < XT:
                    transposes(i + 2)
                if i >= 1:
                    rms_columns(i - 1)
            rms_columns(XT - 1)

            def head(h, last):
                for n in range(INUNITS):
                    pe.wait_ge(w_ready, INUNITS * h + (U_IN + n + 1))
                    for t in range(NT):
                        j = NT * n + t
                        a0, a1 = wide(t) if n in (0, 1, 2, 3) else narrow(t)
                        pe.wait_ge(main_read, G_HEAD * h + (G_IN + j - 2))
                        ins = three(MAIN[t][:, 0:a1 - a0], [
                            (w_hi[:, n % 2, P * k:P * k + P], w_lo[:, n % 2, P * k:P * k + P], x_hi[:, k, a0:a1], x_lo[:, k, a0:a1]) for k in range(KT)])
                        ins.then_inc(main_done, 1)
                        if 8 <= j <= 16:
                            c = j - 8
                            c0 = P * c
                            tail = c == XT - 1
                            rows = TAIL if tail else P
                            pe.wait_ge(masked, 9 * h + c + 1)
                            if c:
                                pe.wait_ge(S_ready, 9 * h + c)
                            if c:
                                pe.wait_ge(o_read, 9 * h + c)
                            vc = v_tail[0:rows, :] if tail else v[:, c, bass.ds(h * P, P)]
                            if tail:
                                wait_alone(pe, vtail_ready, h + 1)
                            o1 = m_.matmul(O_B[0:rows, 0:P], s_msk[0:rows, c % 2, 0:rows], vc, start=True, stop=c == 0)
                            if c:
                                o1 = m_.matmul(O_B[0:rows, 0:P], q_dec[:, c0:c0 + rows], S[:, :], start=False, stop=True)
                            o1.then_inc(o_done, 1)
                            pe.wait_ge(ktok_ready, 9 * h + c + 1)
                            if c == 0:
                                pe.wait_ge(y_ready, 4 * h + 4)
                            m_.matmul(S_B[:, 0:P], k_tok[0:rows, c % 2, :], vc, start=True, stop=True).then_inc(Sinc_done, 1)
                        if 7 <= j <= 15:
                            c = j - 7
                            c0 = P * c
                            rows = P if c < XT - 1 else TAIL
                            if c == 0:
                                pe.wait_ge(q_ready, h + 1)
                                pe.wait_ge(y_ready, 4 * h + 4)
                            else:
                                pe.wait_ge(masked, 9 * h + c)
                                pe.wait_ge(ktok_ready, 9 * h + c)
                            m_.matmul(SC_B[0:rows, 0:rows], k_rot[:, c0:c0 + rows], q_dec[:, c0:c0 + rows], start=True, stop=True)
                            m_.transpose(KT_B[0:rows, 0:P], k_rot[:, c0:c0 + rows], ident[:, :]).then_inc(score_done, 1)
                        if j == 16:
                            pe.wait_ge(state_new, h + 1)
                            pe.wait_ge(smp_std, h + 1)
                            for b in range(SAMPLES):
                                ins = m_.matmul(SMP_B[:, b:b + 1], state[:, b, :], q_rot[:, PROMPT + b:PROMPT + b + 1], start=True, stop=True)
                            ins.then_inc(smp_done, 1)
                pe.wait_ge(smp_sq, h + 1)
                m_.matmul(SMP_B[:, 16:16 + SAMPLES], ones[:, :], sq_smp, start=True, stop=True).then_inc(smp_sum, 1)
                pe.wait_ge(o_normed, h + 1)
                pe.wait_ge(S_ready, 9 * h + 9)
                for c in range(XT):
                    rows = P if c < XT - 1 else TAIL
                    dst = (SC_B, KT_B, S_B)[c // 4][:, P * (c % 4):P * (c % 4) + rows]
                    ins = m_.transpose(dst, o_tok[0:rows, c, :], ident[0:rows, 0:rows])
                    if c % 4 == 3 or c == XT - 1:
                        ins.then_inc(yT_done, 1)

            with pe.Fori(0, HEADS - 1) as h:
                head(h, False)
            head(HEADS - 1, True)

            pe.wait_ge(ctail_done, HEADS)
            pe.wait_ge(smp_std, HEADS + 1)
            for h in range(HEADS):
                ins = m_.transpose(SMP_B[0:2 + SAMPLES, P * h:P * h + P], c_tail[:, h, :], ident[:, :])
            ins.then_inc(ctailT_done, 1)

            def w_pairs(slot, src_hi, src_lo, a0, a1, ktiles=KT, width=P, n0=0):
                return [(w_hi[:, slot, width * k + n0:width * k + n0 + P], w_lo[:, slot, width * k + n0:width * k + n0 + P],
                         src_hi[:, k, a0:a1], src_lo[:, k, a0:a1]) for k in range(ktiles)]

            def out_pair(j):
                for n in range(2):
                    pe.wait_ge(w_ready, 2 * j + (U_OUT + n + 1))
                    for t in range(NT):
                        pe.wait_ge(main_read, 6 * j + (G_OUT + NT * n + t - 2))
                        waits = {}
                        if n == 0:
                            waits = {0: (ylo_done, 1), KT - 1: (ylo_done, 2)} if t == 0 else {0: (ylo_done, t + 2)}
                        three(MAIN[t][:, 0:TW], w_pairs(n, y_hi, y_lo, *narrow(t)), waits).then_inc(main_done, 1)

            with pe.Fori(0, KT // 2) as j:
                out_pair(j)
            pe.wait_ge(y_ready, 4 * HEADS + 4)
            for t in range(NT):
                pe.wait_ge(ssq_done, (KT - 1) * NT + t + 2)
                m_.matmul((O_B, SC_B, KT_B)[t][:, 0:TW], ones[:, :], ssq_h[:, t * TW:(t + 1) * TW], start=True, stop=True).then_inc(sum_done, 1)

            def mlp(b):
                for m in range(8):
                    pe.wait_ge(w_ready, 8 * b + (U_MLP + m + 1))
                    if m < MID:
                        for t in range(NT):
                            pe.wait_ge(main_read, G_BLOCK * b + (G_MLP + NT * m + t - 2))
                            waits = {0: (hlo_done, NT * (KT - 1)), KT - 1: (hlo_done, NT * (KT - 1) + t + 1)} if m == 0 else {}
                            three(MAIN[t][:, 0:TW], w_pairs(m % 2, x_hi, x_lo, *narrow(t)), waits).then_inc(main_done, 1)
                    else:
                        for nn in range(2):
                            for t in range(NT):
                                n = 2 * (m - MID) + nn
                                pe.wait_ge(main_read, G_BLOCK * b + (G_MLP + NT * MID + NT * n + t - 2))
                                waits = {0: (mid_ready, 12 * b + (NT * (MID - 1) + t + 1))} if n == 0 else {}
                                three(MAIN[t][:, 0:TW], w_pairs(m % 2, mid_hi, mid_lo, t * TW, (t + 1) * TW, MID, 2 * P, P * nn), waits).then_inc(main_done, 1)

            with pe.Fori(0, BLOCKS) as b:
                mlp(b)
            for i in range(SEQ // P + 1):
                pe.wait_ge(main_read, G_MLP + BLOCKS * G_BLOCK)
                rows = P if i < SEQ // P else SAMPLES
                c0 = META + P * i
                if i >= 2:
                    pe.wait_ge(f_ready, i - 1)
                for n in range(KT):
                    ins = m_.transpose(XT_B[i % 2][n // 4][0:rows, P * (n % 4):P * (n % 4) + P], acc[:, n, c0:c0 + rows], ident[:, :])
                    if n % 4 == 3:
                        ins.then_inc(fT_done, 1)


def tables():
    f = np.float32
    inv = (f(1) / np.power(f(10000), np.arange(0, DK, 2, dtype=f) / f(DK))).astype(f)
    pos = np.concatenate([np.arange(PROMPT, dtype=f), np.full(SAMPLES, PAST, f)])
    ang = (pos[None, :] * inv[:, None]).astype(f)
    cos, sin = np.cos(ang).astype(f), np.sin(ang).astype(f)
    gamma = np.exp(np.log(f(1) - f(2) ** (f(-5) - np.arange(HEADS, dtype=f))).astype(f)).astype(np.float64)
    i = np.arange(P)
    mask_t = np.zeros((P, HEADS, P))
    dec_t = np.zeros((P, HEADS, P))
    hsc_t = np.zeros((P, HEADS, 8))
    for h, g in enumerate(gamma):
        mask_t[:, h, :] = np.where(i[None, :] >= i[:, None], g ** -(1.0 + i[:, None]), 0.0) * SCALE
        dec_t[:, h, :] = g ** (i[None, :] + 1.0)
        hsc_t[:, h, GAM] = g
        hsc_t[:, h, GAMP] = g ** P
        hsc_t[:, h, GAMT] = g ** TAIL
        hsc_t[:, h, KDEC] = g ** (P - 1.0 - i) * SCALE
        hsc_t[:TAIL, h, KDECT] = g ** (TAIL - 1.0 - i[:TAIL]) * SCALE
    return {
        "ident": np.eye(P, dtype=f),
        "cos_t": np.concatenate([cos, cos]),
        "sin_t": np.concatenate([sin, -sin]),
        "mask_t": mask_t.astype(f),
        "dec_t": dec_t.astype(f),
        "hsc_t": hsc_t.astype(f),
    }


_INS = ["x_prompt", "x_sample", "cache_conv", "state_ret", "meta_tokens", "norm_mix", "w_in", "conv_w",
        "w_out", "norm_mlp", "w_up", "w_down", "norm_final"]
_OUTS = {
    "y_prompt": (1, SEQ, D),
    "y_sample": (SAMPLES, 1, D),
    "new_conv_prompt": (1, 1, 2, CH),
    "new_ret_prompt": (1, 1, HEADS, DK, DK),
    "new_conv_sample": (1, SAMPLES, 2, CH),
    "new_ret_sample": (1, SAMPLES, HEADS, DK, DK),
}


def kernel(**inputs):
    import concourse.bacc as bacc
    from concourse.bass_utils import run_bass_kernel_spmd

    nc = bacc.Bacc("TRN2", target_bir_lowering=False, num_devices=1)
    arrays, io = {}, {}
    for name in _INS:
        arrays[name + "_dram"] = np.ascontiguousarray(inputs[name])
    for name, a in tables().items():
        arrays[name + "_dram"] = np.ascontiguousarray(a)
    for name, a in arrays.items():
        io[name[:-5]] = nc.dram_tensor(name, a.shape, mybir.dt.from_np(a.dtype), kind="ExternalInput").ap()
    for name, shape in _OUTS.items():
        io[name] = nc.dram_tensor(name + "_dram", shape, F32, kind="ExternalOutput").ap()
    io["v_smp"] = nc.dram_tensor("v_smp_dram", (SAMPLES, CH), F32, kind="Internal").ap()
    program(nc, io)
    r = run_bass_kernel_spmd(nc, [arrays], core_ids=[0])
    return tuple(r.results[0][name + "_dram"] for name in _OUTS)
```

```python
from contextlib import ExitStack

import concourse.bass as bass
import numpy as np
from concourse import mybir
from concourse.alu_op_type import AluOpType as ALU

F32 = mybir.dt.float32
F32R = mybir.dt.float32r
ACT = mybir.ActivationFunctionType

P = 128
D = 1024
META = 16
SEQ = 1024
SAMPLES = 8
PAST = 8192
HEADS = 4
DFF = 4 * D
EPS = 1e-6
DK = 128
KT = D // P
PROMPT = META + SEQ
COLS = PROMPT + SAMPLES
XT = -(-COLS // P)
LAST = COLS - (XT - 1) * P
TAIL = PROMPT - (XT - 1) * P
NT = 3
TW = (COLS - META) // NT
START = [META + TW * t for t in range(NT)]
MID = 4
BLOCKS = DFF // (MID * P)
INUNITS = 6
CH = D // 2
SCALE = float(DK) ** -0.5
U0, C0, B0, Q0, K0, V0, G0 = (4 * i for i in range(7))
GMIX, GMLP, CW, CACHE = 0, KT, 2 * KT, 2 * KT + 12
PROWS = CACHE + SAMPLES * 2 * 4
GAM, GAMP, GAMT, KDEC, KDECT = range(5)
G_IN = 2 * XT
G_HEAD = INUNITS * NT
G_OUT = G_IN + HEADS * G_HEAD
G_MLP = G_OUT + KT * NT
G_BLOCK = MID * NT + KT * NT
U_IN = 4
U_OUT = U_IN + HEADS * INUNITS
U_MLP = U_OUT + KT
LOADS_OUT = [1 + 2 * HEADS] * 3 + [1]
LOADS_MLP = [LOADS_OUT[0] + KT // 2, LOADS_OUT[1] + KT // 2, LOADS_OUT[2], LOADS_OUT[3]]


def wide(t, first=0):
    return (first, START[0] + TW) if t == 0 else (START[t], START[t] + TW)


CONV0 = META - 2


def unit_cols(n, t):
    return wide(t) if n < 2 else wide(t, CONV0) if n < 4 else narrow(t)


def narrow(t):
    return START[t], START[t] + TW


WARM = (7, 12)

FULL = (COLS - META) // P
ODD = META + (FULL - 2) * P
FINAL = [(META + P * i, META + P * i + P) for i in range(FULL - 2)] + [(ODD, COLS - 2 * P), (COLS - 2 * P, COLS - P), (COLS - P, COLS)]
LAST_COLS = [(META, META + 3 * P), (META + 3 * P, COLS - 2 * P), (COLS - 2 * P, COLS)]
WHOLE = [0, 0, 0, 1, 1, 1, 1, 2, 2]
TURN = [(9, 9), (11, 11), (13, 13), (16, 16), (17, 17), (19, 19), (20, 20), (22, 23), (23, 23)]
NORM = [10, 12, 14, 17, 18, 20, 21, 23, 23]


def chunk_step(half):
    return half - 15 if 15 <= half <= 15 + XT else None


def tok(i):
    return P * i, min(P * i + P, COLS)


def program(nc, io):
    ctx = ExitStack()
    with ctx:
        place = [16512]

        def at(name, shape, dt, offset):
            return nc.alloc_sbuf_tensor_at(name, [P, *shape], dt, offset=offset)

        def region(size):
            here = place[0]
            place[0] = here + -(-size // 32) * 32
            assert place[0] <= 229344, place[0]
            return here

        def sem(name):
            return ctx.enter_context(nc.semaphore(name))

        W4 = 4 * COLS
        a = region(2 * KT * W4)
        x_hi = at("x_hi", [KT, COLS], F32R, a)
        x_lo = at("x_lo", [KT, COLS], F32R, a + KT * W4)
        y = region(KT * W4)
        wv_hi = at("wv_hi", [KT, CH], F32R, y)
        wv_lo = at("wv_lo", [KT, CH], F32R, y + KT * CH * 4)
        y_raw = at("y_raw", [KT, COLS], F32, y)
        y_lo = at("y_lo", [KT, COLS], F32R, y)
        mid_hi = at("mid_hi", [MID, NT * TW], F32R, y)
        mid_lo = at("mid_lo", [MID, NT * TW], F32R, y + MID * NT * TW * 4)
        o = region(XT * CH * 4 + 4 * W4)
        v = at("v", [XT, CH], F32, o)
        k_rot = at("k_rot", [COLS], F32, o + XT * CH * 4)
        q_rot = at("q_rot", [COLS], F32, o + XT * CH * 4 + W4)
        cosr = at("cosr", [COLS], F32, o + XT * CH * 4 + 2 * W4)
        sinr = at("sinr", [COLS], F32, o + XT * CH * 4 + 3 * W4)
        y_hi = at("y_hi", [KT, COLS], F32R, o)
        acc = at("acc", [KT, COLS], F32, o)
        w = region(4 * 4096)
        w_raw = at("w_raw", [4, 1024], F32, w)
        w_hi = at("w_hi", [2, 1024], F32R, region(2 * 4096))
        w_lo = at("w_lo", [2, 1024], F32R, region(2 * 4096))
        wx_hi = at("wx_hi", [2, 1024], F32R, a)
        wx_lo = at("wx_lo", [2, 1024], F32R, a + 2 * 4096)
        rstd_b = at("rstd_b", [COLS], F32, region(W4))
        t = region(3 * W4 + XT * P * 4 + 2 * 4096)
        x_raw = at("x_raw", [3, D], F32, t)
        cu = at("cu", [COLS], F32, t)
        u_n = at("u_n", [COLS], F32, t + W4)
        o_tok = at("o_tok", [XT, P], F32, t + 2 * W4)
        q_dec = at("q_dec", [COLS], F32, t + 2 * W4 + XT * P * 4)
        state = at("state", [SAMPLES, P], F32, t + 3 * W4 + XT * P * 4)
        v_bc = at("v_bc", [SAMPLES, P], F32, t + 3 * W4 + XT * P * 4 + 4096)
        h_f32 = at("h_f32", [2, TW], F32, t)
        h_sq = at("h_sq", [2, TW], F32, t + 8 * TW)
        ssq_h = at("ssq_h", [NT * TW], F32, t + 16 * TW)
        gain_f = at("gain_f", [D], F32, t + 16 * TW + 4 * NT * TW)
        y_out = at("y_out", [2, D], F32, t + 16 * TW + 4 * NT * TW + 4096)
        r1, r2 = region(8 * (START[0] + TW)), region(8 * (START[0] + TW))
        rot1 = at("rot1", [2, START[0] + TW], F32, r1)
        rot2 = at("rot2", [2, START[0] + TW], F32, r2)
        diag = at("diag", [2, P], F32, r1)
        prm_raw = at("prm_raw", [P], F32, r2)
        c_rows = at("c_rows", [CH], F32, r1)
        k_tok = at("k_tok", [2, P], F32, w + 3 * 4096)
        s_msk = at("s_msk", [2, P], F32, w + 3 * 4096 + 1024)
        v_tail = at("v_tail", [P], F32, w + 3 * 4096 + 2048)
        o_smp = at("o_smp", [P], F32, w + 3 * 4096 + 2560)
        q_smp = at("q_smp", [SAMPLES, SAMPLES], F32, w + 3 * 4096 + 3072)
        S = at("S", [P], F32, region(512))
        mask = at("mask", [HEADS, P], F32, region(2048))
        dec = at("dec", [HEADS, P], F32, region(2048))
        hsc = at("hsc", [HEADS, 8], F32, region(128))
        ident = at("ident", [P], F32, region(512))
        ones = at("ones", [P], F32, region(512))
        prm = at("prm", [PROWS], F32, region(4 * PROWS))
        small = at("small", [104], F32, region(416))
        eps = small[:, 0:1]
        ssq_x, std_x, rstd_x = small[:, 1:10], small[:, 10:19], small[:, 19:28]
        ms_o, std_o, rstd_o = small[:, 28:38], small[:, 38:48], small[:, 48:58]
        k_smp = small[:, 58:66]
        ssq_f, ms_f, std_f, rstd_f = small[:, 96:98], small[:, 98:100], small[:, 100:102], small[:, 102:104]
        c_tail = at("c_tail", [HEADS, 2 + SAMPLES], F32, region(160))

        bank = [ctx.enter_context(nc.psum_tensor(f"bank{i}", [P, 512], F32)) for i in range(8)]
        MAIN = bank[0:3]
        O_B, SC_B, KT_B, S_B, SMP_B = bank[3:8]
        XT_B = [(bank[3], bank[4]), (bank[5], bank[6])]

        x_in = [sem(f"x_in{i}") for i in range(3)]
        raw_in = [sem(f"raw_in{i}") for i in range(4)]
        ident_in, prm_in, tab_in, rope_in = sem("ident_in"), sem("prm_in"), sem("tab_in"), sem("rope_in")
        vs_out, state_in, vbc_in, gain_in = sem("vs_out"), sem("state_in"), sem("vbc_in"), sem("gain_in")
        state_out, S_out, conv_out = sem("state_out"), sem("S_out"), sem("conv_out")
        y_stored = [sem("y_stored0"), sem("y_stored1")]
        const_set, prm_t, prm_ready = sem("const_set"), sem("prm_t"), sem("prm_ready")
        xT_done, xhi_done, xlo_done = sem("xT_done"), sem("xhi_done"), sem("xlo_done")
        ssqx_done, stdx_done, rstdx_done, diag_done = sem("ssqx_done"), sem("stdx_done"), sem("rstdx_done"), sem("diag_done")
        rope_ready = sem("rope_ready")
        w_gained, w_high, w_ready = sem("w_gained"), sem("w_high"), sem("w_ready")
        main_done, main_read = sem("main_done"), sem("main_read")
        rot_added, q_ready, u_ready, gate_ready = sem("rot_added"), sem("q_ready"), sem("u_ready"), sem("gate_ready")
        conv_done = sem("conv_done")
        score_done, masked, ktok_ready = sem("score_done"), sem("masked"), sem("ktok_ready")
        o_done, o_read, Sinc_done, S_ready = sem("o_done"), sem("o_read"), sem("Sinc_done"), sem("S_ready")
        std_ready, o_normed, yT_done, y_ready = sem("std_ready"), sem("o_normed"), sem("yT_done"), sem("y_ready")
        ksmp_ready, state_dec, state_new = sem("ksmp_ready"), sem("state_dec"), sem("state_new")
        smp_done, smp_read, qsmp_set, qsmp_ready = sem("smp_done"), sem("smp_read"), sem("qsmp_set"), sem("qsmp_ready")
        silu_done, vtail_ready = sem("silu_done"), sem("vtail_ready")
        yhi_done, ylo_done = sem("yhi_done"), sem("ylo_done")
        ctail_done, ctailT_done, crows_ready = sem("ctail_done"), sem("ctailT_done"), sem("crows_ready")
        h_ready, hhi_done, hlo_done, hsq_done, ssq_done = sem("h_ready"), sem("hhi_done"), sem("hlo_done"), sem("hsq_done"), sem("ssq_done")
        sum_done, std2_done, rstd2_done = sem("sum_done"), sem("std2_done"), sem("rstd2_done")
        msq_done, mhi_done, mid_ready, acc_set = sem("msq_done"), sem("mhi_done"), sem("mid_ready"), sem("acc_set")
        fT_done, fsq_done, fms_done, fstd_done, frstd_done, f_ready = (sem(n) for n in (
            "fT_done", "fsq_done", "fms_done", "fstd_done", "frstd_done", "f_ready"))
        dve_own, passed = sem("dve_own"), sem("passed")

        def wait_alone(engine, semaphore, value):
            engine.wait_ge(semaphore, value)
            engine.sem_inc(passed, 1)

        w_in_t = io["w_in"][0].rearrange("(k p) n -> p k n", p=P)
        w_out_t = io["w_out"][0].rearrange("(k p) n -> p k n", p=P)
        w_up_t = io["w_up"][0].rearrange("(k p) n -> p k n", p=P)
        w_down_t = io["w_down"][0].rearrange("(k p) n -> p k n", p=P)
        xp, xs, meta = io["x_prompt"][0], io["x_sample"], io["meta_tokens"]
        IN_TILES = [K0, Q0, U0, C0, G0, B0]
        K_ORDER = [k for k in range(KT) if k != HEADS - 1] + [HEADS - 1]

        def raw_loaded_in(h, n):
            return 16 * (2 + n // 3) + 32 * h

        def raw_loaded_mlp(b, m):
            return 16 * (LOADS_MLP[m % 4] + m // 4 + 1) + 32 * b

        def unit(slot, ktiles):
            return w_raw[:, slot, :].rearrange("p (k n) -> p k n", k=ktiles)

        block = ctx.enter_context(nc.Block())

        @block.sync
        def _(sp):
            def load_x(i):
                if i >= 3:
                    sp.wait_ge(xlo_done, 2 * (i - 2))
                    sp.wait_ge(ssqx_done, i - 2)
                s = i % 3
                if i == 0:
                    sp.dma_start(x_raw[META:P, s, :], xp[0:P - META, :]).then_inc(x_in[s], 16)
                    sp.dma_start(x_raw[0:META, s, :], meta).then_inc(x_in[s], 16)
                elif i == XT - 1:
                    sp.dma_start(x_raw[0:TAIL, s, :], xp[SEQ - TAIL:SEQ, :]).then_inc(x_in[s], 16)
                    sp.dma_start(x_raw[TAIL:LAST, s, :], xs.rearrange("b s d -> (b s) d")).then_inc(x_in[s], 16)
                else:
                    sp.dma_start(x_raw[:, s, :], xp[P * i - META:P * i - META + P, :]).then_inc(x_in[s], 16)

            load_x(0)
            sp.dma_start(ident[:, :], io["ident"]).then_inc(ident_in, 16)

            def load_v(u):
                sp.dma_start(unit(u, 2), w_in_t[:, 2 * u:2 * u + 2, V0 * P:(V0 + 4) * P]).then_inc(raw_in[u], 16)

            load_v(0)
            sp.dma_start(prm_raw[GMIX:GMIX + KT, :], io["norm_mix"].rearrange("l (k p) -> (l k) p", p=P)).then_inc(prm_in, 16)
            sp.dma_start(prm_raw[GMLP:GMLP + KT, :], io["norm_mlp"].rearrange("l (k p) -> (l k) p", p=P)).then_inc(prm_in, 16)
            sp.dma_start(prm_raw[CW:CW + 12, :], io["conv_w"].rearrange("l r (c p) -> (l r c) p", p=P)).then_inc(prm_in, 16)
            sp.dma_start(prm_raw[CACHE:PROWS, :], io["cache_conv"].rearrange("l b r (c p) -> (l b r c) p", p=P)).then_inc(prm_in, 16)
            load_v(1)
            load_v(2)
            load_v(3)
            load_x(1)
            load_x(2)
            for i in range(3, XT):
                load_x(i)
            sp.dma_start(cosr[:, :], io["cos_t"]).then_inc(rope_in, 16)
            sp.dma_start(sinr[:, :], io["sin_t"]).then_inc(rope_in, 16)
            sp.dma_start(mask[:, :, :], io["mask_t"]).then_inc(tab_in, 16)
            sp.dma_start(dec[:, :, :], io["dec_t"]).then_inc(tab_in, 16)
            sp.dma_start(hsc[:, :, :], io["hsc_t"]).then_inc(tab_in, 16)
            sp.dma_start(io["new_conv_sample"][0, :, 0, :], io["cache_conv"][0, :, 1, :]).then_inc(conv_out, 16)
            with sp.Fori(0, HEADS) as h:
                for n in range(INUNITS):
                    wait_alone(sp, w_ready, INUNITS * h + (U_IN + n - 2))
                    sp.dma_start(unit(n % 3, KT), w_in_t[:, :, bass.ds(h * P + IN_TILES[n] * P, P)]).then_inc(raw_in[n % 3], 16)
                    if n == 3:
                        wait_alone(sp, y_ready, 3 * h + 3)
                        wait_alone(sp, state_out, 16 * h + 16)
                        sp.wait_ge(vs_out, 16)
                        sp.dma_start(state[:, :, :], io["state_ret"][0, :, bass.ds(h, 1), :, :].rearrange("b h d e -> d (b h) e")).then_inc(state_in, 16)
                        sp.dma_start(v_bc[:, :, :], io["v_smp"][:, bass.ds(h * P, P)].unsqueeze(0).to_broadcast([P, SAMPLES, P])).then_inc(vbc_in, 16)
            with sp.Fori(0, KT // 2) as j:
                for n in range(2):
                    wait_alone(sp, w_ready, 2 * j + (U_OUT + n - 1))
                    sp.dma_start(unit(n, KT), w_out_t[:, :, bass.ds(j * 2 * P + n * P, P)]).then_inc(raw_in[n], 16)

            def load_mlp(b, m, split):
                wait_alone(sp, w_ready, split)
                if m < MID:
                    src = w_up_t[:, :, bass.ds(b * MID * P + m * P, P)]
                    sp.dma_start(unit(m % 4, KT), src).then_inc(raw_in[m % 4], 16)
                else:
                    src = w_down_t[:, bass.ds(b * MID, MID), 256 * (m - MID):256 * (m - MID) + 256]
                    sp.dma_start(unit(m % 4, MID), src).then_inc(raw_in[m % 4], 16)

            for m in range(8):
                load_mlp(0, m, U_MLP + m - 1 if m < 2 else U_MLP + m - 3)
            sp.wait_ge(rstd2_done, NT)
            sp.wait_ge(state_out, 16 * HEADS + 16)
            sp.dma_start(gain_f[:, :], io["norm_final"].unsqueeze(0).to_broadcast([P, D])).then_inc(gain_in, 16)
            with sp.Fori(1, BLOCKS) as b:
                for m in range(8):
                    load_mlp(b, m, 8 * b + (U_MLP + m - 3))
            for i, (c0, c1) in enumerate(FINAL):
                sp.wait_ge(f_ready, i + 1)
                rows = min(c1, PROMPT) - c0
                sp.dma_start(io["y_prompt"][0, c0 - META:c0 - META + rows, :], y_out[0:rows, i % 2, :]).then_inc(y_stored[i % 2], 16)
                if c1 == COLS:
                    sp.dma_start(io["y_sample"].rearrange("b s d -> (b s) d"), y_out[rows:rows + SAMPLES, i % 2, :]).then_inc(y_stored[i % 2], 16)
            sp.wait_ge(y_stored[0], 16 * 6)
            sp.wait_ge(y_stored[1], 16 * 4)
            sp.wait_ge(conv_out, 48)
            sp.wait_ge(state_out, 16 * HEADS + 16)
            sp.wait_ge(S_out, 16 * HEADS + 16)

        @block.gpsimd
        def _(pool):
            g = nc.gpsimd

            def gain(slot, loaded, gtile, ktiles=KT, k0=0):
                pool.wait_ge(raw_in[slot], loaded)
                wt = unit(slot, ktiles)
                gb = prm[:, gtile + k0:gtile + k0 + ktiles].unsqueeze(2).to_broadcast([P, ktiles, 1024 // ktiles])
                g.tensor_tensor(wt, wt, gb, ALU.mult).then_inc(w_gained, 1)

            pool.wait_ge(prm_ready, 1)
            for n in range(2):
                gain(n, raw_loaded_in(0, n), GMIX)
            pool.wait_ge(rope_in, 32)
            pool.wait_ge(main_read, G_IN)
            g.tensor_tensor(cosr[:, :], cosr[:, :], rstd_b[:, :], ALU.mult)
            g.tensor_tensor(sinr[:, :], sinr[:, :], rstd_b[:, :], ALU.mult).then_inc(rope_ready, 1)
            pool.wait_ge(w_ready, U_IN)
            g.memset(q_smp[:, :, :], 0.0).then_inc(qsmp_set, 1)

            def head(h, last):
                for n in range(INUNITS):
                    if n + 2 < INUNITS:
                        gain((n + 2) % 3, raw_loaded_in(h, n + 2), GMIX)
                    elif not last:
                        gain((n + 2) % 3, raw_loaded_in(h + 1, n + 2 - INUNITS), GMIX)
                    if n < 2:
                        for t in range(NT):
                            pool.wait_ge(main_read, G_HEAD * h + (G_IN + NT * n + t + 1))
                            a0, a1 = wide(t)
                            s = (NT * n + t) % 2
                            dst = (k_rot, q_rot)[n]
                            g.tensor_tensor(dst[:, a0:a1], rot1[:, s, 0:a1 - a0], rot2[:, s, 0:a1 - a0], ALU.add).then_inc(rot_added, 1)
                    if n == 1:
                        pool.wait_ge(rot_added, 6 * h + 6)
                        pool.wait_ge(tab_in, 48)
                        full = (XT - 1) * P
                        g.tensor_tensor(q_dec[:, 0:full].rearrange("p (c i) -> p c i", i=P),
                                        q_rot[:, 0:full].rearrange("p (c i) -> p c i", i=P),
                                        dec[:, bass.ds(h, 1), :].to_broadcast([P, XT - 1, P]), ALU.mult)
                        g.tensor_tensor(q_dec[:, full:full + TAIL].unsqueeze(1), q_rot[:, full:full + TAIL].unsqueeze(1),
                                        dec[:, bass.ds(h, 1), 0:TAIL], ALU.mult).then_inc(q_ready, 1)
                    if n == 2:
                        for t in range(NT):
                            pool.wait_ge(main_read, G_HEAD * h + (G_IN + NT * n + t + 1))
                            a0, a1 = unit_cols(n, t)
                            g.tensor_tensor(u_n[:, a0:a1], u_n[:, a0:a1], rstd_b[:, a0:a1], ALU.mult).then_inc(u_ready, 1)
                    if n == 4:
                        pool.wait_ge(conv_done, h + 1)
                        yc = y_raw[:, bass.ds(h, 1), META:COLS]
                        g.tensor_tensor(yc, yc, rstd_b[:, META:COLS].unsqueeze(1), ALU.mult).then_inc(gate_ready, 1)

            with pool.Fori(0, HEADS - 1) as h:
                head(h, False)
            head(HEADS - 1, True)

            pool.wait_ge(y_ready, 3 * HEADS + 3)
            g.memset(ssq_h[:, :], 0.0).then_inc(ssq_done, 1)

            def squares(j, last):
                for i in range(2 * NT):
                    if last and i == 1:
                        gain(0, raw_loaded_mlp(0, 0), GMLP)
                    pool.wait_ge(hsq_done, 6 * j + i + 1)
                    pool.wait_ge(ssq_done, 6 * j + i + 1)
                    c0 = (i % NT) * TW
                    g.tensor_tensor(ssq_h[:, c0:c0 + TW], ssq_h[:, c0:c0 + TW], h_sq[:, i % 2, :], ALU.add).then_inc(ssq_done, 1)
            with pool.Fori(0, KT // 2 - 1) as j:
                squares(j, False)
            squares(KT // 2 - 1, True)
            gain(1, raw_loaded_mlp(0, 1), GMLP)
            pool.wait_ge(main_done, G_MLP)
            pool.wait_ge(hlo_done, KT * NT)
            for n in range(KT):
                if n == 2 or n == 5:
                    gain(2 + n // 5, raw_loaded_mlp(0, 2 + n // 5), GMLP)
                g.tensor_tensor(acc[:, n, META:COLS], x_hi[:, n, META:COLS], x_lo[:, n, META:COLS], ALU.add).then_inc(acc_set, 1)
            with pool.Fori(1, BLOCKS) as b:
                for m in range(MID):
                    gain(m, raw_loaded_mlp(b, m), GMLP)

        @block.scalar
        def _(act):
            s = nc.scalar

            def high(slot, dst_slot, used, dst=w_hi):
                if used is not None:
                    act.wait_ge(main_done, used)
                s.activation(dst[:, dst_slot, :], w_raw[:, slot, :], ACT.Copy).then_inc(w_high, 1)

            act.sem_inc(state_out, 16)
            act.sem_inc(S_out, 16)

            def x_high(i):
                c0, c1 = tok(i)
                for hf in range(2):
                    act.wait_ge(xT_done, 2 * i + hf + 1)
                    src = XT_B[i % 2][hf][:, :].rearrange("p (k c) -> p k c", c=P)[:, :, 0:c1 - c0]
                    s.activation(x_hi[:, 4 * hf:4 * hf + 4, c0:c1], src, ACT.Copy).then_inc(xhi_done, 1)

            for i in range(XT):
                rows = tok(i)[1] - tok(i)[0]
                if i != 1:
                    x_high(i)
                if i == 0:
                    act.wait_ge(prm_t, 1)
                    s.activation(prm[:, :], SMP_B[:, 0:PROWS], ACT.Copy).then_inc(prm_ready, 1)
                    act.wait_ge(prm_ready, 1)
                    for u in range(U_IN):
                        act.wait_ge(raw_in[u], 16)
                        for k in (2 * u, 2 * u + 1):
                            ins = s.activation(wv_hi[:, k, :], unit(u, 2)[:, k % 2, :], ACT.Copy, scale=prm[:, GMIX + k:GMIX + k + 1])
                        ins.then_inc(w_high, 1)
                    x_high(1)
                act.wait_ge(x_in[i % 3], 16 * (i // 3 + 1) + 16 * (i % 3 == 0) + 16 * (i == XT - 1))
                s.activation(q_dec[0:rows, 0:D], x_raw[0:rows, i % 3, :], ACT.Square, accum_out=ssq_x[0:rows, i:i + 1]).then_inc(ssqx_done, 1)
                act.wait_ge(ssqx_done, i + 1)
                if i == 0:
                    act.wait_ge(const_set, 2)
                s.activation(std_x[0:rows, i:i + 1], ssq_x[0:rows, i:i + 1], ACT.Sqrt, scale=1.0 / D, bias=eps[0:rows, :]).then_inc(stdx_done, 1)
            act.wait_ge(w_gained, 1)
            high(0, 0, None)
            act.wait_ge(main_read, G_IN - 2)
            act.dma_start(io["v_smp"], v[TAIL:LAST, XT - 1, :]).then_inc(vs_out, 16)

            def retention(h, step):
                if step:
                    c = step - 1
                    rows = P if c < XT - 1 else TAIL
                    act.wait_ge(o_done, 9 * h + c + 1)
                    s.activation(o_tok[0:rows, c, :], O_B[0:rows, 0:P], ACT.Copy)
                    s.activation(O_B[0:rows, P:2 * P], O_B[0:rows, 0:P], ACT.Square, accum_out=ms_o[0:rows, c:c + 1]).then_inc(o_read, 1)
                    act.wait_ge(o_read, 9 * h + c + 1)
                if step < XT:
                    c = step
                    rows = P if c < XT - 1 else TAIL
                    kd = KDEC if c < XT - 1 else KDECT
                    wait_alone(act, score_done, 9 * h + c + 1)
                    s.activation(k_tok[0:rows, c % 2, :], KT_B[0:rows, 0:P], ACT.Copy,
                                 scale=hsc[0:rows, bass.ds(h, 1), kd:kd + 1].rearrange("p a b -> p (a b)")).then_inc(ktok_ready, 1)

            def y_high(parts, t):
                a0, a1 = narrow(t)
                for k0, k1 in parts:
                    ins = s.activation(y_hi[:, k0:k1, a0:a1], y_raw[:, k0:k1, a0:a1], ACT.Copy)
                ins.then_inc(yhi_done, 1)

            def head(h, last):
                for n in range(INUNITS):
                    if n + 1 < INUNITS or not last:
                        act.wait_ge(w_gained, INUNITS * h + n + 2)
                    else:
                        act.wait_ge(raw_in[0], 16 * (LOADS_OUT[0] + 1))
                    high((n + 1) % 3 if n + 1 < INUNITS else 0, (n + 1) % 2, G_HEAD * h + (G_IN + NT * n))
                    for t in range(NT):
                        j = NT * n + t
                        if chunk_step(2 * j) is not None:
                            retention(h, chunk_step(2 * j))
                        if j == 4:
                            act.wait_ge(rot_added, 6 * h + 3)
                            s.activation(k_smp, k_rot[:, PROMPT:COLS], ACT.Copy, scale=SCALE).then_inc(ksmp_ready, 1)
                            s.activation(v_tail[0:TAIL, :].unsqueeze(1), v[0:TAIL, XT - 1:XT, bass.ds(h * P, P)], ACT.Copy).then_inc(vtail_ready, 1)
                        if j == 5:
                            wait_alone(act, state_in, 16 * h + 16)
                            s.activation(state[:, :, :], state[:, :, :], ACT.Copy,
                                         scale=hsc[:, bass.ds(h, 1), GAM:GAM + 1].rearrange("p a b -> p (a b)")).then_inc(state_dec, 1)
                        if j == 6:
                            act.wait_ge(rot_added, 6 * h + 6)
                            act.wait_ge(qsmp_set, 1)
                            s.activation(q_smp[:, :, :].rearrange("p a b -> p (a b)")[:, 0:SAMPLES * SAMPLES:SAMPLES + 1],
                                         q_rot[:, PROMPT:COLS], ACT.Copy).then_inc(qsmp_ready, 1)
                        if chunk_step(2 * j + 1) is not None:
                            retention(h, chunk_step(2 * j + 1))
                        if j == 8:
                            act.wait_ge(state_new, h + 1)
                            act.dma_start(io["new_ret_sample"][0, :, bass.ds(h, 1), :, :].rearrange("b h d e -> d (b h) e"), state[:, :, :]).then_inc(state_out, 16)
                        if j == 12:
                            act.wait_ge(smp_done, h + 1)
                            s.activation(o_smp[0:SAMPLES, :], SMP_B[0:SAMPLES, 0:P], ACT.Copy)
                            s.activation(SMP_B[0:SAMPLES, P:2 * P], SMP_B[0:SAMPLES, 0:P], ACT.Square, accum_out=ms_o[0:SAMPLES, XT:XT + 1]).then_inc(smp_read, 1)
                            act.wait_ge(smp_read, h + 1)
                            s.activation(std_o[:, 0:XT - 1], ms_o[:, 0:XT - 1], ACT.Sqrt, scale=1.0 / DK, bias=eps)
                            s.activation(std_o[0:TAIL, XT - 1:XT], ms_o[0:TAIL, XT - 1:XT], ACT.Sqrt, scale=1.0 / DK, bias=eps[0:TAIL, :])
                            s.activation(std_o[0:SAMPLES, XT:XT + 1], ms_o[0:SAMPLES, XT:XT + 1], ACT.Sqrt, scale=1.0 / DK, bias=eps[0:SAMPLES, :]).then_inc(std_ready, 1)
                            act.wait_ge(S_ready, 9 * h + 9)
                            act.dma_start(io["new_ret_prompt"][0, 0, bass.ds(h, 1), :, :].rearrange("h d e -> (h d) e"), S[:, :]).then_inc(S_out, 16)
                        if n == 4:
                            a0, a1 = narrow(t)
                            wait_alone(act, main_read, G_HEAD * h + (G_IN + j + 1))
                            yg = y_raw[:, bass.ds(4 + h, 1), a0:a1]
                            s.activation(yg, yg, ACT.Silu).then_inc(silu_done, 1)
                if last:
                    most, rest = ((0, HEADS - 1), (HEADS, KT)), ((HEADS - 1, HEADS),)
                    act.wait_ge(y_ready, 3 * h + 6)
                    y_high(most, 0)
                    y_high(most, 1)
                    act.wait_ge(main_read, G_HEAD * h + (G_IN + NT * 5 + 1))
                    y_high(rest, 0)
                    y_high(most, 2)
                    for t in (1, 2):
                        act.wait_ge(main_read, G_HEAD * h + (G_IN + NT * 5 + t + 1))
                        y_high(rest, t)

            with act.Fori(0, HEADS - 1) as h:
                head(h, False)
            head(HEADS - 1, True)

            act.wait_ge(ctailT_done, 1)
            s.activation(c_rows[0:2 + SAMPLES, :], SMP_B[0:2 + SAMPLES, :], ACT.Copy).then_inc(crows_ready, 1)
            act.wait_ge(crows_ready, 1)
            act.dma_start(io["new_conv_prompt"][0, 0, :, :], c_rows[0:2, :]).then_inc(conv_out, 16)
            act.dma_start(io["new_conv_sample"][0, :, 1, :], c_rows[2:2 + SAMPLES, :]).then_inc(conv_out, 16)

            def out_pair(j, last):
                for n in range(2):
                    if n == 0:
                        act.wait_ge(raw_in[1], 16 * j + 16 * (LOADS_OUT[1] + 1))
                        high(1, 1, 6 * j + G_OUT)
                    elif not last:
                        act.wait_ge(raw_in[0], 16 * j + 16 * (LOADS_OUT[0] + 2))
                        high(0, 0, 6 * j + (G_OUT + NT))
                    else:
                        act.wait_ge(w_gained, HEADS * INUNITS + 1)
                        high(0, 0, 6 * j + (G_OUT + NT))
                    for t in range(NT):
                        i = NT * n + t
                        a0, a1 = narrow(t)
                        wait_alone(act, h_ready, 6 * j + i + 1)
                        s.activation(x_hi[:, bass.ds(2 * j + n, 1), a0:a1], h_f32[:, i % 2, :].unsqueeze(1), ACT.Copy).then_inc(hhi_done, 1)
                        if i >= 2:
                            act.wait_ge(ssq_done, 6 * j + i)
                        else:
                            act.wait_ge(ssq_done, 6 * j + 1)
                        s.activation(h_sq[:, i % 2, :], h_f32[:, i % 2, :], ACT.Square).then_inc(hsq_done, 1)

            with act.Fori(0, KT // 2 - 1) as j:
                out_pair(j, False)
            out_pair(KT // 2 - 1, True)
            def mlp(b, first, last):
                done = G_BLOCK * b + G_MLP
                for m in range(MID if last else 8):
                    nxt = (m + 1) % 8
                    if nxt < MID:
                        act.wait_ge(w_gained, 4 * b + (HEADS * INUNITS + (nxt or MID) + 1))
                    else:
                        act.wait_ge(raw_in[nxt % 4], raw_loaded_mlp(b, nxt))
                    high(nxt % 4, nxt % 2, done + (NT * m if m < MID else NT * MID + 2 * NT * (m - MID)))
                    if m < MID:
                        for t in range(NT):
                            i = NT * m + t
                            if first and m == 0:
                                c0 = META + t * TW
                                act.wait_ge(sum_done, t + 1)
                                s.activation(rstd_b[:, c0:c0 + TW], (O_B, SC_B, KT_B)[t][:, 0:TW], ACT.Sqrt, scale=1.0 / D, bias=eps).then_inc(std2_done, 1)
                            if last and i == NT * MID - 1:
                                act.wait_ge(raw_in[1], raw_loaded_mlp(b, 5))
                                high(1, 1, done + NT * MID)
                            act.wait_ge(main_read, done + i + 1)
                            s.activation(h_sq[:, i % 2, :], h_f32[:, i % 2, :], ACT.Square).then_inc(msq_done, 1)
                            act.wait_ge(msq_done, 12 * b + i + 1)
                            s.activation(mid_hi[:, m, t * TW:(t + 1) * TW], h_sq[:, i % 2, :], ACT.Copy).then_inc(mhi_done, 1)
                if last:
                    for m in (6, 7):
                        act.wait_ge(raw_in[m % 4], raw_loaded_mlp(b, m))
                        high(m % 4, m % 2, done + NT * MID, wx_hi)

            mlp(0, True, False)
            with act.Fori(1, BLOCKS - 1) as b:
                mlp(b, False, False)
            mlp(BLOCKS - 1, False, True)

            for i, (c0, c1) in enumerate(FINAL):
                rows = c1 - c0
                for hf in range(2):
                    act.wait_ge(fT_done, 2 * i + hf + 1)
                    s.activation(h_f32[0:rows, :, :].rearrange("p a b -> p (a b)")[:, 0:512], XT_B[i % 2][hf][0:rows, :], ACT.Square, accum_out=ssq_f[0:rows, hf:hf + 1]).then_inc(fsq_done, 1)
                    act.wait_ge(fsq_done, 2 * i + hf + 1)
                    if hf == 0:
                        s.activation(ms_f[0:rows, 0:1], ssq_f[0:rows, 0:1], ACT.Identity, scale=1.0 / D, bias=eps[0:rows, :]).then_inc(fms_done, 1)
                act.wait_ge(fms_done, i + 1)
                if i >= 2:
                    act.wait_ge(frstd_done, i - 1)
                s.activation(std_f[0:rows, i % 2:i % 2 + 1], ssq_f[0:rows, 1:2], ACT.Sqrt, scale=1.0 / D, bias=ms_f[0:rows, 0:1]).then_inc(fstd_done, 1)

        @block.vector
        def _(dve):
            d = nc.vector

            def low(slot, dst_slot, high_count, lo=w_lo, hi=w_hi):
                dve.wait_ge(w_high, high_count)
                d.tensor_tensor(lo[:, dst_slot, :], w_raw[:, slot, :], hi[:, dst_slot, :], ALU.subtract).then_inc(w_ready, 1)

            dve.sem_inc(y_ready, 3)
            d.memset(eps, EPS).then_inc(const_set, 1)
            d.memset(ones[:, :], 1.0).then_inc(const_set, 1)

            def read_v(i):
                rows = tok(i)[1] - tok(i)[0]
                gi = max(2 * i - 1, 0)
                dve.wait_ge(main_done, gi + 1)
                d.tensor_scalar(v[0:rows, i, :], MAIN[gi % 3][0:rows, :], rstd_x[0:rows, i:i + 1], None, ALU.mult).then_inc(main_read, 1)

            def read_r(i):
                c0, c1 = tok(i)
                gi = 2 * i + 2 if i < XT - 1 else 2 * i + 1
                dve.wait_ge(main_done, gi + 1)
                d.tensor_copy(rstd_b[:, c0:c1], MAIN[gi % 3][:, 0:c1 - c0]).then_inc(main_read, 1)

            def row_rms(i):
                rows = tok(i)[1] - tok(i)[0]
                dve.wait_ge(stdx_done, i + 1)
                d.reciprocal(rstd_x[0:rows, i:i + 1], std_x[0:rows, i:i + 1]).then_inc(rstdx_done, 1)
                dve.wait_ge(rstdx_done, i + 1)
                d.tensor_scalar(diag[0:rows, i % 2, 0:rows], ident[0:rows, 0:rows], rstd_x[0:rows, i:i + 1], None, ALU.mult).then_inc(diag_done, 1)

            dve.wait_ge(ident_in, 16)
            def x_low(i):
                c0, c1 = tok(i)
                for hf in range(2):
                    dve.wait_ge(xhi_done, 2 * i + hf + 1)
                    src = XT_B[i % 2][hf][:, :].rearrange("p (k c) -> p k c", c=P)[:, :, 0:c1 - c0]
                    d.tensor_tensor(x_lo[:, 4 * hf:4 * hf + 4, c0:c1], src, x_hi[:, 4 * hf:4 * hf + 4, c0:c1], ALU.subtract).then_inc(xlo_done, 1)

            for i in range(XT):
                if i != 1:
                    x_low(i)
                if i == 0:
                    for u in range(U_IN):
                        dve.wait_ge(w_high, u + 1)
                        for k in (2 * u, 2 * u + 1):
                            ins = d.scalar_tensor_tensor(out=wv_lo[:, k, :], in0=unit(u, 2)[:, k % 2, :], scalar=prm[:, GMIX + k:GMIX + k + 1],
                                                         in1=wv_hi[:, k, :], op0=ALU.mult, op1=ALU.subtract)
                        ins.then_inc(w_ready, 1)
                    x_low(1)
                if i >= 2:
                    read_v(i - 2)
                if i >= 3:
                    read_r(i - 3)
                if i >= 1:
                    row_rms(i - 1)
            read_v(XT - 2)
            read_r(XT - 3)
            row_rms(XT - 1)
            low(0, 0, U_IN + 1)
            read_v(XT - 1)
            read_r(XT - 2)
            read_r(XT - 1)
            dve.wait_ge(rope_ready, 1)
            OWN = 3

            def retention(h, step):
                if step:
                    c = step - 1
                    gp = GAMP if c < XT - 1 else GAMT
                    dve.wait_ge(Sinc_done, 9 * h + c + 1)
                    if c == 0:
                        dve.wait_ge(S_out, 16 * h + 16)
                        d.tensor_copy(S[:, :], S_B[:, 0:P]).then_inc(S_ready, 1)
                    else:
                        dve.wait_ge(S_ready, 9 * h + c)
                        d.scalar_tensor_tensor(out=S[:, :], in0=S[:, :], scalar=hsc[:, bass.ds(h, 1), gp:gp + 1].rearrange("p a b -> p (a b)"),
                                               in1=S_B[:, 0:P], op0=ALU.mult, op1=ALU.add).then_inc(S_ready, 1)
                if step < XT:
                    c = step
                    rows = P if c < XT - 1 else TAIL
                    dve.wait_ge(score_done, 9 * h + c + 1)
                    d.tensor_tensor(s_msk[0:rows, c % 2, 0:rows].unsqueeze(1), SC_B[0:rows, 0:rows].unsqueeze(1), mask[0:rows, bass.ds(h, 1), 0:rows], ALU.mult).then_inc(masked, 1)

            def y_low(parts, t, count):
                a0, a1 = narrow(t)
                dve.wait_ge(yhi_done, count)
                for k0, k1 in parts:
                    ins = d.tensor_tensor(y_lo[:, k0:k1, a0:a1], y_raw[:, k0:k1, a0:a1], y_hi[:, k0:k1, a0:a1], ALU.subtract)
                ins.then_inc(ylo_done, 1)

            def head(h, last):
                own = [0]

                def mine(ins):
                    own[0] += 1
                    ins.then_inc(dve_own, 1)
                    dve.wait_ge(dve_own, OWN * h + own[0])

                most, rest = ((0, HEADS - 1), (HEADS, KT)), ((HEADS - 1, HEADS),)
                for n in range(INUNITS):
                    low((n + 1) % 3 if n + 1 < INUNITS else 0, (n + 1) % 2, INUNITS * h + (U_IN + n + 2))
                    for t in range(NT):
                        j = NT * n + t
                        pb = MAIN[t]
                        a0, a1 = unit_cols(n, t)
                        w = a1 - a0
                        if chunk_step(2 * j) is not None:
                            retention(h, chunk_step(2 * j))
                        if j == 13:
                            dve.wait_ge(std_ready, h + 1)
                            d.reciprocal(rstd_o[:, 0:XT - 1], std_o[:, 0:XT - 1])
                            d.reciprocal(rstd_o[0:TAIL, XT - 1:XT], std_o[0:TAIL, XT - 1:XT])
                            mine(d.reciprocal(rstd_o[0:SAMPLES, XT:XT + 1], std_o[0:SAMPLES, XT:XT + 1]))
                            d.tensor_tensor(o_tok[:, 0:XT - 1, :], o_tok[:, 0:XT - 1, :], rstd_o[:, 0:XT - 1].unsqueeze(2).to_broadcast([P, XT - 1, P]), ALU.mult)
                            d.tensor_scalar(o_tok[0:TAIL, XT - 1, :], o_tok[0:TAIL, XT - 1, :], rstd_o[0:TAIL, XT - 1:XT], None, ALU.mult)
                            d.tensor_scalar(o_smp[0:SAMPLES, :], o_smp[0:SAMPLES, :], rstd_o[0:SAMPLES, XT:XT + 1], None, ALU.mult).then_inc(o_normed, 1)
                        if j == 15:
                            full = (XT - 1) * P
                            dve.wait_ge(silu_done, 3 * h + 3)
                            for i, (c0, c1, yb, p0) in enumerate(((META, 512, SC_B, META), (512, full, KT_B, 0), (full, COLS, S_B, 0))):
                                dve.wait_ge(yT_done, 3 * h + i + 1)
                                yr = y_raw[:, bass.ds(4 + h, 1), c0:c1]
                                d.tensor_tensor(yr, yb[:, p0:p0 + c1 - c0].unsqueeze(1), yr, ALU.mult).then_inc(y_ready, 1)
                        if last and j == 17:
                            y_low(most, 0, 1)
                            y_low(most, 1, 2)
                        dve.wait_ge(main_done, G_HEAD * h + (G_IN + j + 1))
                        if n < 2:
                            sl = j % 2
                            if j >= 2:
                                dve.wait_ge(rot_added, 6 * h + (j - 1))
                            d.tensor_tensor(rot1[:, sl, 0:w], pb[:, 0:w], cosr[:, a0:a1], ALU.mult)
                            d.tensor_tensor(rot2[0:64, sl, 0:w], pb[64:128, 0:w], sinr[64:128, a0:a1], ALU.mult)
                            d.tensor_tensor(rot2[64:128, sl, 0:w], pb[0:64, 0:w], sinr[0:64, a0:a1], ALU.mult).then_inc(main_read, 1)
                        elif n == 2:
                            d.tensor_tensor(u_n[:, a0:a1], pb[:, 0:w], rstd_b[:, a0:a1], ALU.mult).then_inc(main_read, 1)
                        elif n == 3:
                            dve.wait_ge(u_ready, 3 * h + t + 1)
                            d.tensor_tensor(cu[:, a0:a1], pb[:, 0:w], u_n[:, a0:a1], ALU.mult).then_inc(main_read, 1)
                        elif n == 4:
                            d.tensor_tensor(y_raw[:, bass.ds(4 + h, 1), a0:a1], pb[:, 0:TW].unsqueeze(1), rstd_b[:, a0:a1].unsqueeze(1), ALU.mult).then_inc(main_read, 1)
                        else:
                            if t == 0:
                                dve.wait_ge(gate_ready, h + 1)
                            yb = y_raw[:, bass.ds(h, 1), a0:a1]
                            d.tensor_tensor(yb, pb[:, 0:TW].unsqueeze(1), yb, ALU.mult).then_inc(main_read, 1)
                        if j == 6:
                            dve.wait_ge(state_dec, h + 1)
                            dve.wait_ge(vbc_in, 16 * h + 16)
                            dve.wait_ge(ksmp_ready, h + 1)
                            for b in range(SAMPLES):
                                last_b = d.scalar_tensor_tensor(out=state[:, b, :], in0=v_bc[:, b, :], scalar=k_smp[:, b:b + 1], in1=state[:, b, :], op0=ALU.mult, op1=ALU.add)
                            last_b.then_inc(state_new, 1)
                        if chunk_step(2 * j + 1) is not None:
                            retention(h, chunk_step(2 * j + 1))
                        if j == 11:
                            def cw(r):
                                return prm[:, bass.ds(h + (CW + 4 * r), 1)]

                            def cache(r):
                                rows_ = prm[:, CACHE:PROWS].rearrange("p (b r c) -> p r c b", b=SAMPLES, r=2)
                                return rows_[:, r, bass.ds(h, 1), :]
                            dve.wait_ge(main_read, G_HEAD * h + (G_IN + j + 1))
                            yp = y_raw[:, bass.ds(h, 1), META:PROMPT]
                            ys = y_raw[:, bass.ds(h, 1), PROMPT:COLS]

                            def cucols(c0, c1):
                                return cu[:, c0:c1].unsqueeze(1)
                            d.tensor_scalar(yp, cucols(META - 2, PROMPT - 2), cw(0), None, ALU.mult)
                            mine(d.tensor_scalar(ys, cache(0), cw(0), None, ALU.mult))
                            d.scalar_tensor_tensor(out=yp, in0=cucols(META - 1, PROMPT - 1), scalar=cw(1), in1=yp, op0=ALU.mult, op1=ALU.add)
                            mine(d.scalar_tensor_tensor(out=ys, in0=cache(1), scalar=cw(1), in1=ys, op0=ALU.mult, op1=ALU.add))
                            d.tensor_copy(c_tail[:, bass.ds(h, 1), :], cucols(PROMPT - 2, COLS)).then_inc(ctail_done, 1)
                            d.scalar_tensor_tensor(out=yp, in0=cucols(META, PROMPT), scalar=cw(2), in1=yp, op0=ALU.mult, op1=ALU.add)
                            d.scalar_tensor_tensor(out=ys, in0=cucols(PROMPT, COLS), scalar=cw(2), in1=ys, op0=ALU.mult, op1=ALU.add).then_inc(conv_done, 1)
                if last:
                    y_low(rest, 0, 3)
                    y_low(most, 2, 4)
                    y_low(rest, 1, 5)
                    y_low(rest, 2, 6)
                assert own[0] == OWN

            with dve.Fori(0, HEADS - 1) as h:
                head(h, False)
            head(HEADS - 1, True)

            def out_pair(j, last):
                for n in range(2):
                    low((n + 1) % 2, (n + 1) % 2, 2 * j + (U_OUT + n + 2))
                    for t in range(NT):
                        i = NT * n + t
                        a0, a1 = narrow(t)
                        xh = x_hi[:, bass.ds(2 * j + n, 1), a0:a1]
                        xl = x_lo[:, bass.ds(2 * j + n, 1), a0:a1]
                        hb = h_f32[:, i % 2, :].unsqueeze(1)
                        dve.wait_ge(main_done, 6 * j + (G_OUT + i + 1))
                        if i >= 2:
                            dve.wait_ge(hsq_done, 6 * j + (i - 1))
                        else:
                            dve.wait_ge(ssq_done, 6 * j + 1)
                        d.tensor_tensor(hb, MAIN[t][:, 0:TW].unsqueeze(1), xh, ALU.add).then_inc(main_read, 1)
                        dve.wait_ge(main_read, 6 * j + (G_OUT + i + 1))
                        d.tensor_tensor(hb, hb, xl, ALU.add).then_inc(h_ready, 1)
                        dve.wait_ge(hhi_done, 6 * j + i + 1)
                        d.tensor_tensor(xl, hb, xh, ALU.subtract).then_inc(hlo_done, 1)

            with dve.Fori(0, KT // 2 - 1) as j:
                out_pair(j, False)
            out_pair(KT // 2 - 1, True)
            def mlp(b, first, last):
                done = G_BLOCK * b + G_MLP
                for m in range(MID if last else 8):
                    low((m + 1) % 4, (m + 1) % 2, 8 * b + (U_MLP + m + 2))
                    if m < MID:
                        for t in range(NT):
                            i = NT * m + t
                            a0, a1 = narrow(t)
                            if first and m == 0:
                                dve.wait_ge(std2_done, t + 1)
                                d.reciprocal(rstd_b[:, a0:a1], rstd_b[:, a0:a1]).then_inc(rstd2_done, 1)
                                dve.wait_ge(rstd2_done, t + 1)
                            dve.wait_ge(main_done, done + i + 1)
                            d.scalar_tensor_tensor(out=h_f32[:, i % 2, :], in0=MAIN[t][:, 0:TW], scalar=0.0, in1=rstd_b[:, a0:a1],
                                                   op0=ALU.max, op1=ALU.mult).then_inc(main_read, 1)
                            if last and i == NT * MID - 1:
                                low(1, 1, 8 * b + (U_MLP + 5 + 1))
                            dve.wait_ge(mhi_done, 12 * b + i + 1)
                            d.tensor_tensor(mid_lo[:, m, t * TW:(t + 1) * TW], h_sq[:, i % 2, :], mid_hi[:, m, t * TW:(t + 1) * TW], ALU.subtract).then_inc(mid_ready, 1)
                    else:
                        if first and m == MID:
                            dve.wait_ge(acc_set, KT)
                        for nn in range(2):
                            for t in range(NT):
                                a0, a1 = narrow(t)
                                n = 2 * (m - MID) + nn
                                dve.wait_ge(main_done, done + (NT * MID + NT * n + t + 1))
                                d.tensor_tensor(acc[:, n, a0:a1], MAIN[t][:, 0:TW], acc[:, n, a0:a1], ALU.add).then_inc(main_read, 1)

            def final_norm(i):
                rows = FINAL[i][1] - FINAL[i][0]
                dve.wait_ge(fstd_done, i + 1)
                d.reciprocal(rstd_f[0:rows, i % 2:i % 2 + 1], std_f[0:rows, i % 2:i % 2 + 1]).then_inc(frstd_done, 1)
                dve.wait_ge(frstd_done, i + 1)
                if i == 0:
                    dve.wait_ge(gain_in, 16)
                if i >= 2:
                    dve.wait_ge(y_stored[i % 2], 16 * (i // 2))
                for hf in range(2):
                    ins = d.scalar_tensor_tensor(out=y_out[0:rows, i % 2, 512 * hf:512 * hf + 512], in0=XT_B[i % 2][hf][0:rows, :],
                                                 scalar=rstd_f[0:rows, i % 2:i % 2 + 1], in1=gain_f[0:rows, 512 * hf:512 * hf + 512], op0=ALU.mult, op1=ALU.mult)
                ins.then_inc(f_ready, 1)

            mlp(0, True, False)
            with dve.Fori(1, BLOCKS - 1) as b:
                mlp(b, False, False)
            mlp(BLOCKS - 1, False, True)
            g0 = G_MLP + BLOCKS * G_BLOCK - NT * KT
            for gi in range(NT * KT):
                t, n = gi // KT, gi % KT
                if gi < 2:
                    low(2 + gi, gi, 8 * (BLOCKS - 1) + (U_MLP + 6 + gi + 1), wx_lo, wx_hi)
                a0, a1 = LAST_COLS[t]
                dve.wait_ge(main_done, g0 + gi + 1)
                d.tensor_tensor(acc[:, n, a0:a1], MAIN[gi % 3][:, 0:a1 - a0], acc[:, n, a0:a1], ALU.add).then_inc(main_read, 1)
                for i in range(len(FINAL)):
                    if NORM[i] == gi:
                        final_norm(i)

        @block.tensor
        def _(pe):
            m_ = nc.tensor

            def three(out, pairs, waits=None, middle=None):
                for i, (sh, sl, mh, ml) in enumerate(pairs):
                    if waits and i in waits:
                        pe.wait_ge(*waits[i])
                    m_.matmul(out, sh, mh, start=i == 0, stop=False)
                    m_.matmul(out, sh, ml, start=False, stop=False)
                    ins = m_.matmul(out, sl, mh, start=False, stop=i == len(pairs) - 1)
                    if middle and i == len(pairs) // 2 - 1:
                        middle()
                return ins

            def transposes(i):
                c0, c1 = tok(i)
                rows = c1 - c0
                pe.wait_ge(x_in[i % 3], 16 * (i // 3 + 1) + 16 * (i % 3 == 0) + 16 * (i == XT - 1))
                if i >= 2:
                    pe.wait_ge(xlo_done, 2 * i - 2)
                for k in range(KT):
                    ins = m_.transpose(XT_B[i % 2][k // 4][:, P * (k % 4):P * (k % 4) + rows], x_raw[0:rows, i % 3, P * k:P * k + P], ident[0:rows, 0:rows])
                    if k % 4 == 3:
                        ins.then_inc(xT_done, 1)

            def v_rows(i):
                c0, c1 = tok(i)
                gi = max(2 * i - 1, 0)
                pe.wait_ge(xlo_done, 2 * i + 2)
                if gi >= 3:
                    pe.wait_ge(main_read, gi - 2)
                out = MAIN[gi % 3][0:c1 - c0, :]
                for k in range(KT):
                    if i == 0 and k % 2 == 0:
                        if k == KT - 2:
                            transposes(1)
                        pe.wait_ge(w_ready, k // 2 + 1)
                    m_.matmul(out, x_hi[:, k, c0:c1], wv_hi[:, k, :], start=k == 0, stop=False)
                    m_.matmul(out, x_lo[:, k, c0:c1], wv_hi[:, k, :], start=False, stop=False)
                    if k < KT - 1:
                        m_.matmul(out, x_hi[:, k, c0:c1], wv_lo[:, k, :], start=False, stop=False)
                m_.matmul(out, x_hi[:, KT - 1, c0:c1], wv_lo[:, KT - 1, :], start=False, stop=True).then_inc(main_done, 1)

            def rms_columns(i):
                c0, c1 = tok(i)
                rows = c1 - c0
                gi = 2 * i + 2 if i < XT - 1 else 2 * i + 1
                pe.wait_ge(diag_done, i + 1)
                pe.wait_ge(main_read, gi - 2)
                m_.matmul(MAIN[gi % 3][:, 0:rows], ones[0:rows, :], diag[0:rows, i % 2, 0:rows], start=True, stop=True).then_inc(main_done, 1)

            def keep_warm(n):
                for _ in range(n):
                    m_.matmul(MAIN[2][:, 0:P], ones[:, :], ones[:, :], start=True, stop=True)

            pe.wait_ge(const_set, 2)
            keep_warm(WARM[0])
            pe.wait_ge(ident_in, 16)
            transposes(0)
            pe.wait_ge(prm_in, 64)
            m_.transpose(SMP_B[:, 0:PROWS], prm_raw[0:PROWS, :], ident[0:PROWS, 0:PROWS]).then_inc(prm_t, 1)
            keep_warm(WARM[1])
            for i in range(XT):
                v_rows(i)
                if i + 2 < XT:
                    transposes(i + 2)
                if i >= 1:
                    rms_columns(i - 1)
            rms_columns(XT - 1)

            def w_pairs(slot, src_hi, src_lo, a0, a1, order=range(KT), width=P, n0=0, hi=w_hi, lo=w_lo):
                return [(hi[:, slot, width * k + n0:width * k + n0 + P], lo[:, slot, width * k + n0:width * k + n0 + P],
                         src_hi[:, k, a0:a1], src_lo[:, k, a0:a1]) for k in order]

            def retention(h, step):
                if step:
                    c = step - 1
                    c0 = P * c
                    tail = c == XT - 1
                    rows = TAIL if tail else P
                    pe.wait_ge(masked, 9 * h + c + 1)
                    if c:
                        pe.wait_ge(S_ready, 9 * h + c)
                        pe.wait_ge(o_read, 9 * h + c)
                    vc = v_tail[0:rows, :] if tail else v[:, c, bass.ds(h * P, P)]
                    if tail:
                        wait_alone(pe, vtail_ready, h + 1)
                    o1 = m_.matmul(O_B[0:rows, 0:P], s_msk[0:rows, c % 2, 0:rows], vc, start=True, stop=c == 0)
                    if c:
                        o1 = m_.matmul(O_B[0:rows, 0:P], q_dec[:, c0:c0 + rows], S[:, :], start=False, stop=True)
                    o1.then_inc(o_done, 1)
                    pe.wait_ge(ktok_ready, 9 * h + c + 1)
                    m_.matmul(S_B[:, 0:P], k_tok[0:rows, c % 2, :], vc, start=True, stop=True).then_inc(Sinc_done, 1)
                if step < XT:
                    c = step
                    c0 = P * c
                    rows = P if c < XT - 1 else TAIL
                    if c == 0:
                        pe.wait_ge(q_ready, h + 1)
                        pe.wait_ge(y_ready, 3 * h + 3)
                    m_.matmul(SC_B[0:rows, 0:rows], k_rot[:, c0:c0 + rows], q_dec[:, c0:c0 + rows], start=True, stop=True)
                    m_.transpose(KT_B[0:rows, 0:P], k_rot[:, c0:c0 + rows], ident[:, :]).then_inc(score_done, 1)

            def head(h, last):
                for n in range(INUNITS):
                    pe.wait_ge(w_ready, INUNITS * h + (U_IN + n + 1))
                    for t in range(NT):
                        j = NT * n + t
                        a0, a1 = unit_cols(n, t)
                        pe.wait_ge(main_read, G_HEAD * h + (G_IN + j - 2))
                        middle = None
                        if chunk_step(2 * j) is not None:
                            def middle():
                                retention(h, chunk_step(2 * j))
                        three(MAIN[t][:, 0:a1 - a0], w_pairs(n % 2, x_hi, x_lo, a0, a1), middle=middle).then_inc(main_done, 1)
                        if chunk_step(2 * j + 1) is not None:
                            retention(h, chunk_step(2 * j + 1))
                        if j == 12:
                            pe.wait_ge(state_new, h + 1)
                            pe.wait_ge(qsmp_ready, h + 1)
                            for b in range(SAMPLES):
                                ins = m_.matmul(SMP_B[0:SAMPLES, 0:P], q_smp[:, b, :], state[:, b, :], start=b == 0, stop=b == SAMPLES - 1)
                            ins.then_inc(smp_done, 1)
                        if j == 14:
                            pe.wait_ge(o_normed, h + 1)
                            pe.wait_ge(S_ready, 9 * h + 9)
                            for c in range(XT):
                                rows = P if c < XT - 1 else TAIL
                                dst = (SC_B, KT_B, S_B)[c // 4][:, P * (c % 4):P * (c % 4) + rows]
                                ins = m_.transpose(dst, o_tok[0:rows, c, :], ident[0:rows, 0:rows])
                                if c == 3 or c == 7:
                                    ins.then_inc(yT_done, 1)
                            m_.transpose(S_B[:, TAIL:TAIL + SAMPLES], o_smp[0:SAMPLES, :], ident[0:SAMPLES, 0:SAMPLES]).then_inc(yT_done, 1)

            with pe.Fori(0, HEADS - 1) as h:
                head(h, False)
            head(HEADS - 1, True)

            pe.wait_ge(ctail_done, HEADS)
            pe.wait_ge(smp_read, HEADS)
            for h in range(HEADS):
                ins = m_.transpose(SMP_B[0:2 + SAMPLES, P * h:P * h + P], c_tail[:, h, :], ident[:, :])
            ins.then_inc(ctailT_done, 1)

            def out_pair(j):
                for n in range(2):
                    pe.wait_ge(w_ready, 2 * j + (U_OUT + n + 1))
                    for t in range(NT):
                        pe.wait_ge(main_read, 6 * j + (G_OUT + NT * n + t - 2))
                        waits = {0: (ylo_done, (1, 2, 4)[t]), KT - 1: (ylo_done, (3, 5, 6)[t])} if n == 0 else {}
                        three(MAIN[t][:, 0:TW], w_pairs(n, y_hi, y_lo, *narrow(t), K_ORDER), waits).then_inc(main_done, 1)

            with pe.Fori(0, KT // 2) as j:
                out_pair(j)

            def up(b, m, first=False):
                pe.wait_ge(w_ready, 8 * b + (U_MLP + m + 1))
                for t in range(NT):
                    pe.wait_ge(main_read, G_BLOCK * b + (G_MLP + NT * m + t - 2))
                    waits = {0: (hlo_done, NT * (KT - 1)), KT - 1: (hlo_done, NT * (KT - 1) + t + 1)} if first else {}
                    three(MAIN[t][:, 0:TW], w_pairs(m % 2, x_hi, x_lo, *narrow(t)), waits).then_inc(main_done, 1)
                    if first:
                        pe.wait_ge(y_ready, 3 * HEADS + 3)
                        pe.wait_ge(ssq_done, (KT - 1) * NT + t + 2)
                        m_.matmul((O_B, SC_B, KT_B)[t][:, 0:TW], ones[:, :], ssq_h[:, t * TW:(t + 1) * TW], start=True, stop=True).then_inc(sum_done, 1)

            def down(b, m):
                pe.wait_ge(w_ready, 8 * b + (U_MLP + m + 1))
                for nn in range(2):
                    for t in range(NT):
                        n = 2 * (m - MID) + nn
                        pe.wait_ge(main_read, G_BLOCK * b + (G_MLP + NT * MID + NT * n + t - 2))
                        waits = {0: (mid_ready, 12 * b + (NT * (MID - 1) + t + 1))} if n == 0 else {}
                        three(MAIN[t][:, 0:TW], w_pairs(m % 2, mid_hi, mid_lo, t * TW, (t + 1) * TW, range(MID), 2 * P, P * nn), waits).then_inc(main_done, 1)

            def final_transposes(i, hf):
                c0, c1 = FINAL[i]
                pe.wait_ge(main_read, g0 + KT * WHOLE[i] + 4 * hf + 4)
                if i >= 2:
                    pe.wait_ge(f_ready, i - 1)
                for n in range(4 * hf, 4 * hf + 4):
                    ins = m_.transpose(XT_B[i % 2][hf][0:c1 - c0, P * (n % 4):P * (n % 4) + P], acc[:, n, c0:c1], ident[:, :])
                ins.then_inc(fT_done, 1)

            for m in range(MID):
                up(0, m, m == 0)
            for m in range(MID, 8):
                down(0, m)
            with pe.Fori(1, BLOCKS - 1) as b:
                for m in range(MID):
                    up(b, m)
                for m in range(MID, 8):
                    down(b, m)
            for m in range(MID):
                up(BLOCKS - 1, m)
            g0 = G_MLP + BLOCKS * G_BLOCK - NT * KT
            for gi in range(NT * KT):
                t, n = gi // KT, gi % KT
                if t == 0 and n % 2 == 0:
                    pe.wait_ge(w_ready, 8 * (BLOCKS - 1) + (U_MLP + MID + n // 2 + 1))
                pe.wait_ge(main_read, g0 + gi - 2)
                a0, a1 = LAST_COLS[t]
                waits = {0: (mid_ready, 12 * (BLOCKS - 1) + (NT * (MID - 1) + (2 if t == 0 else NT)))} if n == 0 else {}
                where = {"hi": w_hi, "lo": w_lo} if n < 4 else {"hi": wx_hi, "lo": wx_lo}
                three(MAIN[gi % 3][:, 0:a1 - a0], w_pairs(n // 2 % 2, mid_hi, mid_lo, a0 - META, a1 - META, range(MID), 2 * P, P * (n % 2), **where), waits).then_inc(main_done, 1)
                for i in range(len(FINAL)):
                    for hf in range(2):
                        if TURN[i][hf] == gi:
                            final_transposes(i, hf)


def tables():
    f = np.float32
    inv = (f(1) / np.power(f(10000), np.arange(0, DK, 2, dtype=f) / f(DK))).astype(f)
    pos = np.concatenate([np.arange(PROMPT, dtype=f), np.full(SAMPLES, PAST, f)])
    ang = (pos[None, :] * inv[:, None]).astype(f)
    cos, sin = np.cos(ang).astype(f), np.sin(ang).astype(f)
    gamma = np.exp(np.log(f(1) - f(2) ** (f(-5) - np.arange(HEADS, dtype=f))).astype(f)).astype(np.float64)
    i = np.arange(P)
    mask_t = np.zeros((P, HEADS, P))
    dec_t = np.zeros((P, HEADS, P))
    hsc_t = np.zeros((P, HEADS, 8))
    for h, g in enumerate(gamma):
        mask_t[:, h, :] = np.where(i[None, :] >= i[:, None], g ** -(1.0 + i[:, None]), 0.0) * SCALE
        dec_t[:, h, :] = g ** (i[None, :] + 1.0)
        hsc_t[:, h, GAM] = g
        hsc_t[:, h, GAMP] = g ** P
        hsc_t[:, h, GAMT] = g ** TAIL
        hsc_t[:, h, KDEC] = g ** (P - 1.0 - i) * SCALE
        hsc_t[:TAIL, h, KDECT] = g ** (TAIL - 1.0 - i[:TAIL]) * SCALE
    return {
        "ident": np.eye(P, dtype=f),
        "cos_t": np.concatenate([cos, cos]),
        "sin_t": np.concatenate([sin, -sin]),
        "mask_t": mask_t.astype(f),
        "dec_t": dec_t.astype(f),
        "hsc_t": hsc_t.astype(f),
    }


_INS = ["x_prompt", "x_sample", "cache_conv", "state_ret", "meta_tokens", "norm_mix", "w_in", "conv_w",
        "w_out", "norm_mlp", "w_up", "w_down", "norm_final"]
_OUTS = {
    "y_prompt": (1, SEQ, D),
    "y_sample": (SAMPLES, 1, D),
    "new_conv_prompt": (1, 1, 2, CH),
    "new_ret_prompt": (1, 1, HEADS, DK, DK),
    "new_conv_sample": (1, SAMPLES, 2, CH),
    "new_ret_sample": (1, SAMPLES, HEADS, DK, DK),
}


def kernel(**inputs):
    import concourse.bacc as bacc
    from concourse.bass_utils import run_bass_kernel_spmd

    nc = bacc.Bacc("TRN2", target_bir_lowering=False, num_devices=1)
    arrays, io = {}, {}
    for name in _INS:
        arrays[name + "_dram"] = np.ascontiguousarray(inputs[name])
    for name, a in tables().items():
        arrays[name + "_dram"] = np.ascontiguousarray(a)
    for name, a in arrays.items():
        io[name[:-5]] = nc.dram_tensor(name, a.shape, mybir.dt.from_np(a.dtype), kind="ExternalInput").ap()
    for name, shape in _OUTS.items():
        io[name] = nc.dram_tensor(name + "_dram", shape, F32, kind="ExternalOutput").ap()
    io["v_smp"] = nc.dram_tensor("v_smp_dram", (SAMPLES, CH), F32, kind="Internal").ap()
    program(nc, io)
    r = run_bass_kernel_spmd(nc, [arrays], core_ids=[0])
    return tuple(r.results[0][name + "_dram"] for name in _OUTS)
```
